# Optimizing a Trainium2 kernel written in Bass

```python
import jax, jax.numpy as jnp
from jax import lax
import numpy as np

D_MODEL = 1024
BATCH = 1
SEQ = 256
DEPTH = 2

N_BRANCH = 4
MIX_W = 256
SGU_GROUPS = 4
SGU_CHUNK = 128
N_Q_HEADS = 4
N_KV_HEADS = 2
HEAD_DIM = 64
WINDOW = 128
ROT_DIM = HEAD_DIM // 4
ROPE_THETA = 500000.0
SHORT_CONV = 3
CONFORMER_CONV = 31
N_GROUPS = 4
EXPERTS_PER_GROUP = 4
N_EXPERTS = N_GROUPS * EXPERTS_PER_GROUP
TOP_K = 2
D_EXPERT = 256
EPS = 1e-6

IN_WIDTHS = (MIX_W, MIX_W,
             N_Q_HEADS * HEAD_DIM, N_KV_HEADS * HEAD_DIM, N_KV_HEADS * HEAD_DIM,
             MIX_W, MIX_W, MIX_W,
             MIX_W, MIX_W)
D_IN = sum(IN_WIDTHS)

kernel_name = 'hybrid_gated_branches_hier_moe'

def rmsnorm(x, g):
    xf = x.astype(jnp.float32)
    y = xf * lax.rsqrt(jnp.mean(xf * xf, axis=-1, keepdims=True) + EPS)
    return (y * g.astype(jnp.float32)).astype(x.dtype)

def layernorm(x, g, b):
    xf = x.astype(jnp.float32)
    mu = jnp.mean(xf, axis=-1, keepdims=True)
    xc = xf - mu
    var = jnp.mean(xc * xc, axis=-1, keepdims=True)
    y = xc * lax.rsqrt(var + EPS) * g.astype(jnp.float32) + b.astype(jnp.float32)
    return y.astype(x.dtype)

def causal_dwconv(x, w):
    k, c = w.shape
    return lax.conv_general_dilated(x, w[:, None, :], window_strides=(1,), padding=[(k - 1, 0)],
                                    dimension_numbers=('NWC', 'WIO', 'NWC'), feature_group_count=c)

def split_cols(p):
    outs, start = [], 0
    for w in IN_WIDTHS:
        outs.append(p[..., start:start + w])
        start += w
    return outs

def rope_tables(positions):
    inv = ROPE_THETA ** (-jnp.arange(0, ROT_DIM, 2, dtype=jnp.float32) / ROT_DIM)
    ang = positions.astype(jnp.float32)[..., None] * inv
    return jnp.cos(ang)[:, :, None, :], jnp.sin(ang)[:, :, None, :]

def apply_partial_rope(x, cos, sin):
    half = ROT_DIM // 2
    x1 = x[..., :half].astype(jnp.float32)
    x2 = x[..., half:ROT_DIM].astype(jnp.float32)
    rot = jnp.concatenate([x1 * cos - x2 * sin, x2 * cos + x1 * sin], axis=-1).astype(x.dtype)
    return jnp.concatenate([rot, x[..., ROT_DIM:]], axis=-1)

def sgu_mixer(u, v, ln_g, ln_b, w_s, b_s):
    bsz, s, _ = u.shape
    nc = s // SGU_CHUNK
    u = jax.nn.gelu(u)
    v = layernorm(jax.nn.gelu(v), ln_g, ln_b)
    vc = v.reshape(bsz, nc, SGU_CHUNK, SGU_GROUPS, MIX_W // SGU_GROUPS)
    causal = jnp.tril(jnp.ones((SGU_CHUNK, SGU_CHUNK), dtype=bool))
    w = jnp.where(causal[None], w_s, 0)
    z = jnp.einsum('gts,bnsgc->bntgc', w, vc) + b_s.T[None, None, :, :, None]
    return u * z.reshape(bsz, s, MIX_W)

def swa_sink_attention(q, k, v, qn_g, kn_g, sinks, cos, sin):
    bsz, s, _ = q.shape
    nb = s // WINDOW
    grp = N_Q_HEADS // N_KV_HEADS
    q = apply_partial_rope(rmsnorm(q.reshape(bsz, s, N_Q_HEADS, HEAD_DIM), qn_g), cos, sin)
    k = apply_partial_rope(rmsnorm(k.reshape(bsz, s, N_KV_HEADS, HEAD_DIM), kn_g), cos, sin)
    v = v.reshape(bsz, s, N_KV_HEADS, HEAD_DIM)
    qb = q.reshape(bsz, nb, WINDOW, N_KV_HEADS, grp, HEAD_DIM)

    def band(t):
        tb = t.reshape(bsz, nb, WINDOW, N_KV_HEADS, HEAD_DIM)
        prev = jnp.pad(tb, ((0, 0), (1, 0), (0, 0), (0, 0), (0, 0)))[:, :-1]
        return jnp.concatenate([prev, tb], axis=2)

    kb, vb = band(k), band(v)
    sc = jnp.einsum('bnqhgd,bnkhd->bnhgqk', qb, kb, preferred_element_type=jnp.float32) * (HEAD_DIM ** -0.5)
    qi = jnp.arange(WINDOW)[:, None]
    ki = jnp.arange(2 * WINDOW)[None, :]
    diff = qi + WINDOW - ki
    in_win = (diff >= 0) & (diff < WINDOW)
    first = (jnp.arange(nb) == 0)[:, None, None]
    valid = in_win[None] & ~(first & (ki < WINDOW)[None])
    sc = jnp.where(valid[None, :, None, None], sc, -jnp.inf)
    sink = sinks.astype(jnp.float32).reshape(N_KV_HEADS, grp)[None, None, :, :, None, None]
    m = jnp.maximum(jnp.max(sc, axis=-1, keepdims=True), sink)
    p = jnp.exp(sc - m)
    p = p / (jnp.sum(p, axis=-1, keepdims=True) + jnp.exp(sink - m))
    o = jnp.einsum('bnhgqk,bnkhd->bnqhgd', p.astype(vb.dtype), vb)
    return o.reshape(bsz, s, N_Q_HEADS * HEAD_DIM)

def short_conv_mixer(b_gate, c_gate, xin, w3):
    return c_gate * causal_dwconv(b_gate * xin, w3)

def conformer_conv(a, gate, w31, b31, cn_g, cn_b):
    y = a * jax.nn.sigmoid(gate)
    y = causal_dwconv(y, w31) + b31
    return jax.nn.silu(layernorm(y, cn_g, cn_b))

def mixing_block(h, cos, sin, w_in, sgu_ln_g, sgu_ln_b, sgu_w, sgu_b, q_norm_g, k_norm_g, sinks,
                 conv3_w, conv31_w, conv31_b, cnorm_g, cnorm_b, w_branch, w_gate, b_gate, w_o):
    bsz, s, _ = h.shape
    a_u, a_v, b_q, b_k, b_v, c_b, c_c, c_x, d_a, d_g = split_cols(h @ w_in)
    y_a = sgu_mixer(a_u, a_v, sgu_ln_g, sgu_ln_b, sgu_w, sgu_b)
    y_b = swa_sink_attention(b_q, b_k, b_v, q_norm_g, k_norm_g, sinks, cos, sin)
    y_c = short_conv_mixer(c_b, c_c, c_x, conv3_w)
    y_d = conformer_conv(d_a, d_g, conv31_w, conv31_b, cnorm_g, cnorm_b)
    ys = jnp.stack([y_a, y_b, y_c, y_d], axis=2)
    gates = jax.nn.sigmoid(h @ w_gate + b_gate).reshape(bsz, s, N_BRANCH, D_MODEL)
    merged = jnp.einsum('bsnc,ncd,bsnd->bsd', ys, w_branch, gates)
    return merged @ w_o

def hier_moe(h, w_group, b_group, w_expert, b_expert, w_e_gate, w_e_up, w_e_down):
    bsz, s, d = h.shape
    t = h.reshape(-1, d)
    g_logits = (t @ w_group + b_group).astype(jnp.float32)
    g_idx = jnp.argmax(g_logits, axis=-1)
    g_w = jnp.take_along_axis(jax.nn.softmax(g_logits, axis=-1), g_idx[:, None], axis=-1)
    e_logits = (t @ w_expert + b_expert).astype(jnp.float32).reshape(-1, N_GROUPS, EXPERTS_PER_GROUP)
    e_in = jnp.take_along_axis(e_logits, g_idx[:, None, None], axis=1)[:, 0]
    top_v, top_i = lax.top_k(e_in, TOP_K)
    top_w = jax.nn.softmax(top_v, axis=-1) * g_w
    expert_id = g_idx[:, None] * EXPERTS_PER_GROUP + top_i
    combine = jnp.sum(jax.nn.one_hot(expert_id, N_EXPERTS, dtype=jnp.float32) * top_w[..., None], axis=1)
    hid = jax.nn.silu(jnp.einsum('td,edf->tef', t, w_e_gate)) * jnp.einsum('td,edf->tef', t, w_e_up)
    out = jnp.einsum('tef,efd,te->td', hid, w_e_down, combine.astype(t.dtype))
    return out.reshape(bsz, s, d)

def setup_inputs(seed: int = 0) -> dict:
    key = jax.random.key(seed)
    ks = jax.random.split(key, 32)
    L = DEPTH
    f32 = jnp.float32

    def nrm(k, shape, scale):
        return jax.random.normal(k, shape, dtype=f32) * scale

    def gain(k, shape):
        return 1.0 + nrm(k, shape, 0.02)

    return {
        'x': nrm(ks[0], (BATCH, SEQ, D_MODEL), 1.0),
        'positions': jnp.broadcast_to(jnp.arange(SEQ, dtype=jnp.int32)[None], (BATCH, SEQ)),
        'norm1_g': gain(ks[1], (L, D_MODEL)),
        'w_in': nrm(ks[2], (L, D_MODEL, D_IN), D_MODEL ** -0.5),
        'sgu_ln_g': gain(ks[3], (L, MIX_W)),
        'sgu_ln_b': nrm(ks[4], (L, MIX_W), 0.02),
        'sgu_w': nrm(ks[5], (L, SGU_GROUPS, SGU_CHUNK, SGU_CHUNK), SGU_CHUNK ** -0.5),
        'sgu_b': gain(ks[6], (L, SGU_GROUPS, SGU_CHUNK)),
        'q_norm_g': gain(ks[7], (L, HEAD_DIM)),
        'k_norm_g': gain(ks[8], (L, HEAD_DIM)),
        'sinks': nrm(ks[9], (L, N_Q_HEADS), 0.5),
        'conv3_w': nrm(ks[10], (L, SHORT_CONV, MIX_W), SHORT_CONV ** -0.5),
        'conv31_w': nrm(ks[11], (L, CONFORMER_CONV, MIX_W), CONFORMER_CONV ** -0.5),
        'conv31_b': nrm(ks[12], (L, MIX_W), 0.02),
        'cnorm_g': gain(ks[13], (L, MIX_W)),
        'cnorm_b': nrm(ks[14], (L, MIX_W), 0.02),
        'w_branch': nrm(ks[15], (L, N_BRANCH, MIX_W, D_MODEL), MIX_W ** -0.5),
        'w_gate': nrm(ks[16], (L, D_MODEL, N_BRANCH * D_MODEL), D_MODEL ** -0.5),
        'b_gate': nrm(ks[17], (L, N_BRANCH * D_MODEL), 0.02),
        'w_o': nrm(ks[18], (L, D_MODEL, D_MODEL), D_MODEL ** -0.5),
        'norm2_g': gain(ks[19], (L, D_MODEL)),
        'w_group': nrm(ks[20], (L, D_MODEL, N_GROUPS), D_MODEL ** -0.5),
        'b_group': nrm(ks[21], (L, N_GROUPS), 0.01),
        'w_expert': nrm(ks[22], (L, D_MODEL, N_EXPERTS), D_MODEL ** -0.5),
        'b_expert': nrm(ks[23], (L, N_EXPERTS), 0.01),
        'w_e_gate': nrm(ks[24], (L, N_EXPERTS, D_MODEL, D_EXPERT), D_MODEL ** -0.5),
        'w_e_up': nrm(ks[25], (L, N_EXPERTS, D_MODEL, D_EXPERT), D_MODEL ** -0.5),
        'w_e_down': nrm(ks[26], (L, N_EXPERTS, D_EXPERT, D_MODEL), D_EXPERT ** -0.5),
    }

def reference(x, positions, norm1_g, w_in, sgu_ln_g, sgu_ln_b, sgu_w, sgu_b, q_norm_g, k_norm_g, sinks,
              conv3_w, conv31_w, conv31_b, cnorm_g, cnorm_b, w_branch, w_gate, b_gate, w_o,
              norm2_g, w_group, b_group, w_expert, b_expert, w_e_gate, w_e_up, w_e_down):
    cos, sin = rope_tables(positions)
    for l in range(DEPTH):
        h = rmsnorm(x, norm1_g[l])
        x = x + mixing_block(h, cos, sin, w_in[l], sgu_ln_g[l], sgu_ln_b[l], sgu_w[l], sgu_b[l],
                             q_norm_g[l], k_norm_g[l], sinks[l], conv3_w[l], conv31_w[l], conv31_b[l],
                             cnorm_g[l], cnorm_b[l], w_branch[l], w_gate[l], b_gate[l], w_o[l])
        h = rmsnorm(x, norm2_g[l])
        x = x + hier_moe(h, w_group[l], b_group[l], w_expert[l], b_expert[l],
                         w_e_gate[l], w_e_up[l], w_e_down[l])
    return x


_drawn_inputs = setup_inputs


def setup_inputs(seed=0):
    import zlib

    import numpy as np

    out = dict(_drawn_inputs(seed))
    spreads = {}
    factors = {'sgu_ln_g': 20.708,
     'sgu_ln_b': 13.836,
     'q_norm_g': 4.017,
     'k_norm_g': 6.623,
     'sinks': 69.518,
     'cnorm_g': 12.097,
     'cnorm_b': 12.986,
     'b_gate': 3.25,
     'b_group': 90.123,
     'b_expert': 20.924,
     'sgu_b': 5.951,
     'norm2_g': 3.518}
    for name, (base, spread) in spreads.items():
        noise = np.random.default_rng([zlib.crc32(name.encode()), seed]).standard_normal(out[name].shape)
        drawn = base * np.exp(spread * noise) if base else spread * noise
        out[name] = __import__('jax').numpy.asarray(drawn.astype(out[name].dtype))
    for name, factor in factors.items():
        out[name] = (out[name] * factor).astype(out[name].dtype)
    return out
```

```python
from contextlib import ExitStack

import numpy as np

import concourse.bass as bass
from concourse import mybir

F32 = mybir.dt.float32
F32R = mybir.dt.float32r
I32 = mybir.dt.int32
ALU = mybir.AluOpType
ACT = mybir.ActivationFunctionType
AX = mybir.AxisListType.X

P = 128
EPS = 1e-6
ROPE_THETA = 500000.0
NEG = -1.0e30
RAW = 4
PART = 4
UNIT = 2048
DMAS = 2


def trunk(nc, x_in, positions, norm1_g, w_in, sgu_ln_g, sgu_ln_b, sgu_w, sgu_b, q_norm_g, k_norm_g, sinks,
          conv3_w, conv31_w, conv31_b, cnorm_g, cnorm_b, w_branch, w_gate, b_gate, w_o,
          norm2_g, w_group, b_group, w_expert, b_expert, w_e_gate, w_e_up, w_e_down, out):
    DEPTH, D, D_IN = w_in.shape
    SEQ = x_in.shape[1]
    T = SEQ // P
    KT = D // P
    NBR, MIX = w_branch.shape[1], w_branch.shape[2]
    CT = MIX // P
    GS = sgu_w.shape[1]
    HD = q_norm_g.shape[1]
    NQ = sinks.shape[1]
    NKV = (D_IN - 7 * MIX - NQ * HD) // (2 * HD)
    NH = NQ + NKV
    ROT = HD // 4
    HALF = ROT // 2
    K3, K31 = conv3_w.shape[1], conv31_w.shape[1]
    NG = w_group.shape[2]
    NE = w_expert.shape[2]
    EPG = NE // NG
    F = w_e_gate.shape[3]
    FT = F // P
    NR = NG + NE
    assert (T, KT, CT, GS, NQ, NG, EPG, FT) == (2, 8, 2, 4, 4, 4, 4, 2) and SEQ == 256

    units_a = [("in", b, h) for b in range(4) for h in range(2)] + [("in_last", 4, h) for h in range(2)]
    units_a += [("gate", b, h) for b in range(8) for h in range(2)]
    units_a += [("branch", n, 0) for n in range(NBR)]
    units_a += [("out", 0, 2), ("out", 2, 2)] + [("out", k, 1) for k in range(4, KT)]
    units_m = [("gu", 0, 0), ("gu", 0, 1), ("gu", 1, 0), ("gu", 1, 1), ("down", 0, 0), ("gu", 2, 0), ("gu", 2, 1),
               ("down", 1, 0), ("gu", 3, 0), ("gu", 3, 1), ("down", 2, 0), ("down", 3, 0)]
    NA, NM = len(units_a), len(units_m)
    assert all(n % r == 0 for n in (NA, NM) for r in (RAW, PART))
    G0, Y0, O0 = 10, 26, 30
    AHEAD = PART - 1

    def width(n, moe):
        kind, _, h = ("gu", 0, 0) if moe else units_a[n]
        return UNIT // 2 if kind == "in_last" or (kind == "out" and h == 1) else UNIT

    class At:

        def __init__(self, l, passes, moe):
            self.l, self.passes, self.moe = l, passes, moe

        def unit(self, n):
            return (self.l + 1) * NA + self.passes * NM + n if self.moe else self.l * NA + self.passes * NM + n

        def ring(self, n):
            return self.unit(n) + 1

        def slot(self, n, ring):
            return n % ring

        def landed(self, n):
            layers = self.l + 1 if self.moe else self.l
            return 16 * DMAS * (layers * (NA // RAW) + self.passes * (NM // RAW) + n // RAW + 1)

    with ExitStack() as ctx:
        def sb(name, shape, dt=F32):
            return ctx.enter_context(nc.sbuf_tensor(name, shape, dt))

        def sem(name):
            return ctx.enter_context(nc.semaphore(name))

        raw = sb("raw", [P, RAW, UNIT])
        w_hi = sb("w_hi", [P, PART, UNIT], F32R)
        w_lo = sb("w_lo", [P, PART, UNIT], F32R)
        x = sb("x", [P, T, D])
        a_hi = sb("a_hi", [P, 2048], F32R)
        a_lo = sb("a_lo", [P, 2048], F32R)
        xn = sb("xn", [P, T, KT, P])
        gates = sb("gates", [P, 8, T, 512])
        y_hi = sb("y_hi", [P, NBR, CT * SEQ], F32R)
        y_lo = sb("y_lo", [P, NBR, CT * SEQ], F32R)
        u_t = sb("u_t", [P, CT * SEQ])
        v_n = sb("v_n", [P, T, MIX])
        p_t = sb("p_t", [P, 12, P])
        c_gate = sb("c_gate", [P, CT, SEQ])
        c_b = sb("c_b", [P, CT, SEQ])
        bx = sb("bx", [P, CT, K3 - 1 + SEQ])
        dpad = sb("dpad", [P, CT, K31 - 1 + SEQ])
        d_sig = sb("d_sig", [P, CT, SEQ])
        d_acc = sb("d_acc", [P, CT, SEQ])
        y_tmp = sb("y_tmp", [P, CT * SEQ])
        g1 = sb("g1", [P, KT])
        g2 = sb("g2", [P, KT])
        lng = sb("lng", [P, MIX])
        lnb = sb("lnb", [P, MIX])
        sgw_t = sb("sgw_t", [P, GS, P])
        sgb = sb("sgb", [GS, P])
        qg = sb("qg", [P, HD])
        kg = sb("kg", [P, HD])
        snk = sb("snk", [P, NQ])
        NROW = K31 + 3 + K3
        rows = sb("rows", [NROW, MIX])
        cols = sb("cols", [P, CT, NROW])
        bg_hi = sb("bg_hi", [16, 512], F32R)
        bg = sb("bg", [16, 512], F32R)
        wr = sb("wr", [P, KT, NR])
        rb = sb("rb", [NR, 1])
        ident = sb("ident", [P, P])
        ones = sb("ones", [P, P])
        below = sb("below", [P, P])
        upto = sb("upto", [P, P])
        amask = sb("amask", [P, 2 * P])
        iota = sb("iota", [P, 512])
        icol = sb("icol", [P, NG])
        widx = sb("widx", [P, 3, NG])
        sgsel = sb("sgsel", [GS, MIX])
        s12 = sb("s12", [16, 2])
        bsel_f = y_tmp
        bsel = sb("bsel", [16, 8, P], F32R)
        mhalf = sb("mhalf", [P, 16])
        warm = sb("warm", [1, 1])
        posi = sb("posi", [P, T], I32)
        cos_sin = sb("cos_sin", [P, 2, T, HALF])
        ssq = sb("ssq", [P, T])
        rstd = sb("rstd", [P, T])
        v_mu = sb("v_mu", [P, T])
        v_ss = sb("v_ss", [P, T])
        v_rs = sb("v_rs", [P, T])
        qkss = sb("qkss", [P, T * NH])
        qkrs = sb("qkrs", [P, T * NH])
        st = sb("st", [P, 8, T, NQ])
        small = d_acc[:, :, :].rearrange("p c s -> p (c s)")
        at_small = [0]

        def take(n):
            at_small[0] += n
            return small[:, at_small[0] - n:at_small[0]]

        r1 = take(24 * T).rearrange("p (i t) -> p i t", t=T)
        r4 = take(12 * T * NG).rearrange("p (i t g) -> p i t g", t=T, g=NG)
        lg = take(T * NR).rearrange("p (t r) -> p t r", t=T)
        cmf = take(T * 8).rearrange("p (t m) -> p t m", t=T)
        cwf = take(NG * 16).rearrange("p (g m) -> p g m", g=NG)
        cwt = take(2 * NG * EPG).rearrange("p (q e) -> p q e", e=EPG)
        cnt = take(4 * NG).rearrange("p (i g) -> p i g", g=NG)
        pr = take(T * NE).rearrange("p (t g e) -> p t g e", t=T, g=NG)
        cmr = sb("cmr", [P, T, 16], F32R)
        tab_f = sb("tab_f", [P, 3, 8])
        tab = sb("tab", [P, 3, 8], I32)

        h_hi = a_hi[:, :].rearrange("p (k s) -> p k s", k=KT)
        h_lo = a_lo[:, :].rearrange("p (k s) -> p k s", k=KT)
        xt_hi = a_hi[:, :].rearrange("p (t k s) -> p t k s", t=T, k=KT)
        xt_lo = a_lo[:, :].rearrange("p (t k s) -> p t k s", t=T, k=KT)
        g_hi = y_lo[:, 2:4, :].rearrange("p a s -> p (a s)").rearrange("p (k s) -> p k s", k=KT)
        g_lo = y_hi[:, 2:4, :].rearrange("p a s -> p (a s)").rearrange("p (k s) -> p k s", k=KT)
        z_hi, z_lo = a_hi[:, 0:1024], a_lo[:, 0:1024]
        flat_g = gates[:, :, :, :].rearrange("p a t n -> p (a t n)")
        xg = flat_g[:, 0:4096].rearrange("p (k s) -> p k s", k=KT)
        h32 = flat_g[:, 4096:6144].rearrange("p (k s) -> p k s", k=KT)
        sil = flat_g[:, 6144:6144 + 512].rearrange("p (b f) -> p b f", b=2)
        hid = flat_g[:, 6656:6656 + 512].rearrange("p (b f) -> p b f", b=2)
        diag = flat_g[:, 7168:7168 + SEQ].rearrange("p (t s) -> p t s", t=T)
        qkv = flat_g[:, 6144:7168].rearrange("p (t n) -> p t n", t=T)
        qk_t = flat_g[:, 7168:7936].rearrange("p (t n) -> p t n", t=T)
        sel = y_hi[:, 0:2, :].rearrange("p a s -> p (a s)").rearrange("p (t s) -> p t s", t=T)
        sel_t = a_hi[:, 1024:1024 + SEQ]
        hd_hi = y_lo[:, 0, :].rearrange("p (b f s) -> p b f s", b=2, f=FT)
        hd_lo = y_lo[:, 1, :].rearrange("p (b f s) -> p b f s", b=2, f=FT)
        xnf = xn[:, :, :, :].rearrange("p t k s -> p (t k s)")
        merged = xnf.rearrange("p (t d) -> p t d", t=T)
        sc = [xnf[:, 0:512].rearrange("p (h k) -> p h k", h=NQ),
              xnf[:, 512:1536].rearrange("p (h k) -> p h k", h=NQ)]
        p_flat = p_t[:, :, :].rearrange("p a s -> p (a s)")
        qk = p_flat[:, 0:T * NH * HD].rearrange("p (t h d) -> p t h d", t=T, h=NH)
        rope = p_flat[:, 1024:1024 + 4 * T * NH * HALF].rearrange("p (i t h j) -> p i t h j", i=4, t=T, h=NH)
        bg_raw = c_gate[0:16, :, :].rearrange("p c s -> p (c s)")
        sgw = d_sig[:, :, :].rearrange("p c s -> p (c s)").rearrange("p (g s) -> p g s", g=GS)
        lt = y_tmp[0:NR, 0:SEQ]
        posb = y_tmp[:, SEQ:2 * SEQ]
        yc_out = c_gate[:, :, :].rearrange("p c s -> p (c s)")
        dn = [y_tmp[:, 0:SEQ], y_tmp[:, SEQ:2 * SEQ], c_b[:, 0, :]]

        def merged_part(h, q):
            return h[:, 4 * (q % 2):4 * (q % 2) + 4, P * (q // 2):P * (q // 2) + P]

        bank = [ctx.enter_context(nc.psum_tensor(f"bank{i}", [P, 512], F32)) for i in range(8)]

        landed = [sem(f"landed{i}") for i in range(RAW)]
        hi_done = sem("hi_done")
        split_done = sem("split_done")
        unit_used = sem("unit_used")
        x_loaded, pos_loaded = sem("x_loaded"), sem("pos_loaded")
        par_g = sem("par_g")
        par_a, par_r = sem("par_a"), sem("par_r")
        pool_consts = sem("pool_consts")
        stored = sem("stored")
        dve_step = sem("dve_step")

        names = {}

        def S(name):
            if name not in names:
                names[name] = sem(name)
            return names[name]

        DVE_STEPS = 157

        class Steps:
            def __init__(self, eng, s):
                self.eng, self.s, self.n = eng, s, 0
                self.base = 0

            def at(self, base):
                self.base, self.n = base, 0

            def do(self, ins):
                ins.then_inc(self.s, 1)
                self.n += 1
                self.eng.wait_ge(self.s, self.base + self.n)

            def mark(self, ins):
                ins.then_inc(self.s, 1)
                self.n += 1
                return self.n

            def upto(self, n):
                self.eng.wait_ge(self.s, self.base + n)

        block = ctx.enter_context(nc.Block())

        @block.sync
        def _(sp):
            sp.dma_start(posi[:, :], positions[0].rearrange("(t p) -> p t", p=P),
                         allow_slow_non_contiguous=True).then_inc(pos_loaded, 16)
            for t in range(T):
                sp.dma_start(x[:, t, :], x_in[0, P * t:P * t + P, :]).then_inc(x_loaded, 16)

            def norm_gains(l):
                sp.dma_start(g1[:, :], norm1_g[l].rearrange("(p c) -> p c", c=KT)).then_inc(par_g, 16)

            def mixer_parameters(l):
                sp.dma_start(lng[:, :], row(sgu_ln_g, l)).then_inc(par_a, 16)
                sp.dma_start(lnb[:, :], row(sgu_ln_b, l)).then_inc(par_a, 16)
                sp.dma_start(sgw[:, :, :], sgu_w[l].rearrange("g t s -> t g s")).then_inc(par_a, 16)
                sp.dma_start(sgb[:, :], sgu_b[l]).then_inc(par_a, 16)
                sp.dma_start(qg[:, :], row(q_norm_g, l)).then_inc(par_a, 16)
                sp.dma_start(kg[:, :], row(k_norm_g, l)).then_inc(par_a, 16)
                sp.dma_start(snk[:, :], row(sinks, l)).then_inc(par_a, 16)
                r = 0
                for w, k in ((conv31_w, K31), (conv31_b, 1), (cnorm_g, 1), (cnorm_b, 1), (conv3_w, K3)):
                    src = w[l] if k > 1 else w[l].unsqueeze(0)
                    sp.dma_start(rows[r:r + k, :], src).then_inc(par_a, 16)
                    r += k
                bgv = b_gate[l].rearrange("(n c) -> n c", c=512)
                sp.dma_start(bg_raw[0:8, :], bgv).then_inc(par_a, 16)
                sp.dma_start(bg_raw[8:16, :], bgv).then_inc(par_a, 16)

            def row(w, l):
                return w[l].unsqueeze(0).to_broadcast([P, w.shape[1]])

            def router_parameters(l):
                sp.dma_start(wr[:, :, 0:NG], w_group[l].rearrange("(p c) e -> p c e", c=KT)).then_inc(par_r, 16)
                sp.dma_start(wr[:, :, NG:NR], w_expert[l].rearrange("(p c) e -> p c e", c=KT)).then_inc(par_r, 16)
                sp.dma_start(rb[0:NG, :], b_group[l].unsqueeze(1)).then_inc(par_r, 16)
                sp.dma_start(rb[NG:NR, :], b_expert[l].unsqueeze(1)).then_inc(par_r, 16)
                sp.dma_start(g2[:, :], norm2_g[l].rearrange("(p c) -> p c", c=KT)).then_inc(par_r, 16)

            def load(at, n, kind, i, h, l, e=None, table=False):
                slot = at.slot(n, RAW)
                sp.wait_ge(split_done, at.ring(n))
                if table:
                    sp.wait_ge(S("tab_ready"), l + 1)
                dst = raw[:, slot, :]
                for j in range(DMAS):
                    if kind == "in":
                        d = dst.rearrange("p (c m) -> p c m", c=4)[:, 2 * j:2 * j + 2, :]
                        s = w_in[l].rearrange("(p c) m -> p c m", c=KT)[:, 4 * h + 2 * j:4 * h + 2 * j + 2,
                                                                       512 * i:512 * i + 512]
                    elif kind == "in_last":
                        d = dst[:, 0:1024].rearrange("p (c m) -> p c m", c=4)[:, 2 * j:2 * j + 2, :]
                        s = w_in[l].rearrange("(p c) m -> p c m", c=KT)[:, 4 * h + 2 * j:4 * h + 2 * j + 2,
                                                                       512 * i:512 * i + 256]
                    elif kind == "gate":
                        d = dst.rearrange("p (c m) -> p c m", c=4)[:, 2 * j:2 * j + 2, :]
                        s = w_gate[l].rearrange("(p c) m -> p c m", c=KT)[:, 4 * h + 2 * j:4 * h + 2 * j + 2,
                                                                         512 * i:512 * i + 512]
                    elif kind == "branch":
                        d = dst[:, 1024 * j:1024 * j + 1024]
                        s = w_branch[l, i, P * j:P * j + P, :]
                    elif kind == "out":
                        if h == 2:
                            d = dst[:, 1024 * j:1024 * j + 1024]
                            s = w_o[l, P * (i + j):P * (i + j + 1), :]
                        else:
                            d = dst[:, 512 * j:512 * j + 512]
                            s = w_o[l, P * i:P * i + P, 512 * j:512 * j + 512]
                    elif kind == "gu":
                        d = dst[:, 1024 * j:1024 * j + 1024].rearrange("p (c f) -> p c f", c=4)
                        w = (w_e_gate, w_e_up)[j]
                        s = w[l, e].rearrange("(p c) f -> p c f", c=KT)[:, 4 * h:4 * h + 4, :]
                    else:
                        d = dst[:, 1024 * j:1024 * j + 1024]
                        s = w_e_down[l, e, P * j:P * j + P, :]
                    sp.dma_start(d, s).then_inc(landed[slot], 16)

            def first_units(at, l):
                for n in range(AHEAD):
                    load(at, n, *units_a[n], l)

            norm_gains(0)
            first_units(At(0, 0, False), 0)
            mixer_parameters(0)
            router_parameters(0)
            sp.wait_ge(S("tab_zero"), 1)
            with sp.Fori(0, DEPTH) as l:
                before = sp.value_load(tab[0:1, 0, 7:8], min_val=0, max_val=DEPTH * (NG + 1))
                at = At(l, before, False)
                for n in range(AHEAD, NA):
                    load(at, n, *units_a[n], l)
                with sp.Fori(0, NG - 1) as g:
                    at = At(l, before + g, True)
                    for n, (kind, i, h) in enumerate(units_m):
                        load(at, n, kind, i, h, l, g * EPG + i, table=n == NM - 1)
                npass = sp.value_load(tab[0:1, 0, 6:7], min_val=NG, max_val=NG + 1)
                with sp.Fori(NG - 1, npass) as p:
                    g = sp.value_load(tab[0:1, 0, bass.ds(p, 1)], min_val=0, max_val=NG - 1)
                    at = At(l, before + p, True)
                    for n, (kind, i, h) in enumerate(units_m):
                        load(at, n, kind, i, h, l, g * EPG + i)
                nxt = (l + 1) % DEPTH
                first_units(At(l + 1, before + npass, False), nxt)
                sp.wait_ge(S("x_mid"), 4 * (l + 1))
                norm_gains(nxt)
                mixer_parameters(nxt)
                sp.wait_ge(S("gp_hi"), 2 * (before + l) + 2)
                router_parameters(nxt)
            for t in range(T):
                sp.wait_ge(S("x_out"), 2 * T * (DEPTH - 1) + 2 * t + 2)
                sp.dma_start(out[0, P * t:P * t + P, :], x[:, t, :]).then_inc(stored, 16)
            sp.wait_ge(par_a, 16 * 14 * (DEPTH + 1))
            sp.wait_ge(par_g, 16 * (DEPTH + 1))
            sp.wait_ge(par_r, 16 * 5 * (DEPTH + 1))
            sp.wait_ge(stored, 16 * T)

        @block.gpsimd
        def _(pool):
            k = [0]

            def step(ins):
                ins.then_inc(pool_consts, 1)
                k[0] += 1
                pool.wait_ge(pool_consts, k[0])

            g = nc.gpsimd
            step(g.memset(ones[:, :], 1.0))
            step(g.memset(ident[:, :], 0.0))
            step(g.affine_select(out=ident[:, :], in_=ident[:, :], compare_op=ALU.not_equal, fill=1.0, base=0,
                                 pattern=[[-1, P]], channel_multiplier=1))
            step(g.affine_select(out=below[:, :], in_=ones[:, :], compare_op=ALU.is_ge, fill=0.0, base=-1,
                                 pattern=[[1, P]], channel_multiplier=-1))
            step(g.affine_select(out=upto[:, :], in_=ones[:, :], compare_op=ALU.is_ge, fill=0.0, base=0,
                                 pattern=[[1, P]], channel_multiplier=-1))
            step(g.memset(amask[:, :], 0.0))
            step(g.affine_select(out=amask[:, 0:P], in_=amask[:, 0:P], compare_op=ALU.is_ge, fill=NEG, base=-1,
                                 pattern=[[1, P]], channel_multiplier=-1))
            step(g.affine_select(out=amask[:, P:2 * P], in_=amask[:, P:2 * P], compare_op=ALU.is_ge, fill=NEG, base=0,
                                 pattern=[[-1, P]], channel_multiplier=1))
            step(g.iota(iota[:, :], pattern=[[1, 512]], base=0, channel_multiplier=0,
                        allow_small_or_imprecise_dtypes=True))
            step(g.iota(icol[:, :], pattern=[[P, NG]], base=0, channel_multiplier=1,
                        allow_small_or_imprecise_dtypes=True))
            step(g.iota(widx[:, 0, :], pattern=[[-1, NG]], base=NG, channel_multiplier=0,
                        allow_small_or_imprecise_dtypes=True))
            step(g.iota(widx[:, 1, :], pattern=[[1, NG]], base=0, channel_multiplier=0,
                        allow_small_or_imprecise_dtypes=True))
            step(g.iota(widx[:, 2, :], pattern=[[1, NG]], base=1, channel_multiplier=0,
                        allow_small_or_imprecise_dtypes=True))
            step(g.memset(widx[:, 2, NG - 1:NG], 0.0))
            step(g.memset(sgsel[:, :], 1.0))
            w = MIX // GS
            step(g.affine_select(out=sgsel[:, :], in_=sgsel[:, :], compare_op=ALU.is_ge, fill=0.0, base=0,
                                 pattern=[[1, MIX]], channel_multiplier=-w))
            step(g.affine_select(out=sgsel[:, :], in_=sgsel[:, :], compare_op=ALU.is_ge, fill=0.0, base=w - 1,
                                 pattern=[[-1, MIX]], channel_multiplier=w))
            step(g.memset(s12[:, 0:1], 1.0))
            step(g.memset(s12[:, 1:2], 0.0))
            step(g.affine_select(out=s12[:, 0:1], in_=s12[:, 0:1], compare_op=ALU.is_ge, fill=-1.0, base=7,
                                 pattern=[[0, 1]], channel_multiplier=-1))
            step(g.affine_select(out=s12[:, 1:2], in_=s12[:, 1:2], compare_op=ALU.is_ge, fill=1.0, base=7,
                                 pattern=[[0, 1]], channel_multiplier=-1))
            step(g.memset(mhalf[:, :], -0.5))
            def power(ready, dst, src, width, done, l):
                pool.wait_ge(S(ready), l + 1)
                g.tensor_tensor(dst, src, mhalf[:, 0:width], ALU.pow).then_inc(S(done), 1)

            for half in range(2):
                v = bsel_f[0:16, 0:512].rearrange("p (b s) -> p b s", b=4)
                if half:
                    power("n1_ms", rstd[:, :], ssq[:, :], T, "n1_rs", 0)
                    pool.wait_ge(S("bsel_copied"), 1)
                step(g.memset(v, 0.0))
                for off in (0, 8):
                    step(g.affine_select(out=v, in_=v, compare_op=ALU.not_equal, fill=1.0, base=-off - 4 * half,
                                         pattern=[[-1, 4], [0, P]], channel_multiplier=1))

            with pool.Fori(0, DEPTH) as l:
                power("v_ms", v_rs[:, :], v_ss[:, :], T, "v_rs_done", l)
                power("qk_ms", qkrs[:, :], qkss[:, :], T * NH, "qk_rs", l)
                power("n2_ms", rstd[:, :], ssq[:, :], T, "n2_rs", l)
                power("n1_ms", rstd[:, :], ssq[:, :], T, "n1_rs", l + 1)
            pool.drain()

        @block.scalar
        def _(act):
            a = nc.scalar

            def hi(at, n):
                slot = at.slot(n, RAW)
                act.wait_ge(landed[slot], at.landed(n))
                act.wait_ge(unit_used, at.ring(n))
                w = width(n, at.moe)
                a.activation(w_hi[:, at.slot(n, PART), 0:w], raw[:, slot, 0:w], ACT.Copy).then_inc(hi_done, 1)

            def used(at, n):
                act.wait_ge(unit_used, at.unit(n) + PART + 1)

            def pass_tokens(half, slot):
                a.activation(g_hi[:, 4 * half:4 * half + 4, :], xg[:, 4 * half:4 * half + 4, bass.ds(slot, P)],
                             ACT.Copy).then_inc(S("gp_hi"), 1)

            def scale_rows(l, n, t):
                act.wait_ge(S(n + "_rs"), l + 1)
                a.activation(xn[:, t, :, :], x[:, t, :].rearrange("q (p c) -> q c p", c=KT), ACT.Identity,
                             scale=rstd[:, t:t + 1]).then_inc(S(n + "_xa"), 1)

            act.wait_ge(S("angles"), 1)
            a.activation(cos_sin[:, :, :, :], rope[:, 0, 0:2, 0:2, :], ACT.Sin).then_inc(S("rope_ready"), 1)
            def square(t):
                a.activation(xn[:, t, :, :].rearrange("p k s -> p (k s)"), x[:, t, :], ACT.Square,
                             accum_out=ssq[:, t:t + 1]).then_inc(S("n1_ssq"), 1)

            act.wait_ge(x_loaded, 16 * T)
            for t in range(T):
                square(t)
            hi(At(0, 0, False), 0)
            scale_rows(0, "n1", 0)
            for n in range(1, AHEAD):
                hi(At(0, 0, False), n)
            act.wait_ge(S("tab_zero"), 1)
            with act.Fori(0, DEPTH) as l:
                before = act.value_load(tab[0:1, 0, 7:8], min_val=0, max_val=DEPTH * (NG + 1))
                at = At(l, before, False)
                act.wait_ge(par_g, 16 * (l + 1))
                for k in range(KT):
                    act.wait_ge(S("n1_t"), 4 * l + k // 2 + 1)
                    a.activation(h_hi[:, k, :], bank[4 + k // 2][:, 256 * (k % 2):256 * (k % 2) + 256], ACT.Identity,
                                 scale=g1[:, k:k + 1]).then_inc(S("h_hi_done"), 1)
                act.wait_ge(par_a, 16 * 14 * (l + 1))
                a.activation(bg_hi[:, :], bg_raw[:, :], ACT.Copy).then_inc(S("bg_hi_done"), 1)
                for n in range(AHEAD, 6):
                    hi(at, n)
                used(at, 1)
                a.activation(u_t[:, :], bank[0][:, :], ACT.Gelu_apprx_tanh).then_inc(S("win_act"), 1)
                for t in range(T):
                    last = a.activation(v_n[:, t, :], bank[1][:, MIX * t:MIX * t + MIX], ACT.Gelu_apprx_tanh,
                                        accum_out=v_mu[:, t:t + 1])
                last.then_inc(S("win_act"), 1)
                hi(at, 6)
                hi(at, 7)
                used(at, 3)
                for t in range(T):
                    a.activation(qkv[:, t, :], bank[2 + t][:, :], ACT.Copy).then_inc(S("win_act"), 1)
                hi(at, 8)
                hi(at, 9)
                hi(at, 10)
                used(at, 5)
                a.activation(c_b[:, :, :].rearrange("p c s -> p (c s)"), bank[0][:, :], ACT.Copy).then_inc(S("win_act"), 1)
                a.activation(c_gate[:, :, :].rearrange("p c s -> p (c s)"), bank[1][:, :],
                             ACT.Copy).then_inc(S("win_act"), 1)
                hi(at, 11)
                hi(at, 12)
                hi(at, 13)
                used(at, 9)
                a.activation(d_sig[:, :, :].rearrange("p c s -> p (c s)"), bank[0][:, :],
                             ACT.Sigmoid).then_inc(S("win_act"), 1)

                def gate(b):
                    used(at, G0 + 2 * b + 1)
                    for t in range(T):
                        if b == 6 and t == 0:
                            act.wait_ge(S("o_done"), l + 1)
                        a.activation(gates[:, b, t, :], bank[(2 * b + t + 1) % 4][:, :],
                                     ACT.Sigmoid).then_inc(S("gates_done"), 1)

                hi(at, 14)
                for t in range(T):
                    act.wait_ge(S("qk_tp"), T * l + t + 1)
                    a.activation(qk_t[:, t, :], bank[6 + t][:, 0:384], ACT.Copy).then_inc(S("qk_t_done"), 1)
                hi(at, 15)
                gate(0)
                hi(at, 16)
                hi(at, 17)
                gate(1)
                act.wait_ge(S("mx_done"), l + 1)
                for t in range(T):
                    for h in range(NQ):
                        a.activation(sc[t][:, h, :], sc[t][:, h, :], ACT.Exp, bias=st[:, 1, t, h:h + 1],
                                     accum_out=st[:, 2, t, h:h + 1]).then_inc(S("exp_done"), 1)
                a.activation(st[:, 4, :, :].rearrange("p t h -> p (t h)"), st[:, 3, :, :].rearrange("p t h -> p (t h)"),
                             ACT.Exp).then_inc(S("exp_done"), 1)
                hi(at, 18)
                hi(at, 19)
                gate(2)
                hi(at, 20)
                hi(at, 21)
                gate(3)
                for i, b in enumerate((7, 4, 5)):
                    act.wait_ge(S("p_tp"), 3 * l + i + 1)
                    a.activation(p_t[:, 4 * i:4 * i + 4, :].rearrange("p a s -> p (a s)"), bank[b][:, :],
                                 ACT.Copy).then_inc(S("p_t_done"), 1)
                hi(at, 22)
                act.wait_ge(S("ya_done"), l + 1)
                a.activation(y_hi[:, 0, :], u_t[:, :], ACT.Copy).then_inc(S("y_hi_done"), 1)
                act.wait_ge(S("yc_done"), l + 1)
                a.activation(y_hi[:, 2, :], yc_out, ACT.Copy).then_inc(S("y_hi_done"), 1)
                hi(at, 23)
                gate(4)
                act.wait_ge(S("o_done"), l + 1)
                a.activation(y_hi[:, 1, :], bank[6][:, :], ACT.Copy).then_inc(S("y_hi_done"), 1)
                hi(at, 24)
                hi(at, 25)
                gate(5)
                hi(at, 26)
                act.wait_ge(S("dc_done"), l + 1)
                a.activation(d_sig[:, :, :].rearrange("p c s -> p (c s)"), d_acc[:, :, :].rearrange("p c s -> p (c s)"),
                             ACT.Square).then_inc(S("dsq_done"), 1)
                hi(at, 27)
                gate(6)
                hi(at, 28)
                gate(7)
                hi(at, 29)
                act.wait_ge(S("dv_done"), l + 1)
                a.activation(dn[1], dn[0], ACT.Ln).then_inc(S("dln_done"), 1)
                act.wait_ge(S("dln_done"), l + 1)
                a.activation(dn[1], dn[1], ACT.Exp, scale=-0.5).then_inc(S("dr0_done"), 1)
                act.wait_ge(S("dx_done"), l + 1)
                for c in range(CT):
                    a.activation(d_sig[:, c, :], d_acc[:, c, :], ACT.Silu, bias=cols[:, c, K31 + 2:K31 + 3],
                                 scale=cols[:, c, K31 + 1:K31 + 2]).then_inc(S("yd_done"), 1)
                act.wait_ge(S("yd_done"), CT * (l + 1))
                a.activation(y_hi[:, 3, :], d_sig[:, :, :].rearrange("p c s -> p (c s)"), ACT.Copy).then_inc(S("y_hi_done"), 1)
                for n in range(30, 33):
                    hi(at, n)
                for q in range(4):
                    act.wait_ge(S("m_tp"), 4 * l + q + 1)
                    a.activation(merged_part(h_hi, q), bank[q][:, :].rearrange("p (k s) -> p k s", k=4),
                                 ACT.Copy).then_inc(S("m_hi_done"), 1)
                for n in range(33, NA):
                    hi(at, n)
                at = At(l, before, True)
                hi(at, 0)
                hi(at, 1)
                for t in range(T):
                    act.wait_ge(S("x_mid"), 4 * l + 2 * t + 2)
                    a.activation(xn[:, t, :, :].rearrange("p k s -> p (k s)"), x[:, t, :], ACT.Square,
                                 accum_out=ssq[:, t:t + 1]).then_inc(S("n2_ssq"), 1)
                scale_rows(l, "n2", 0)
                act.wait_ge(par_r, 16 * 5 * (l + 1))
                for k in (0, 1, 4, 5):
                    act.wait_ge(S("n2_t"), 4 * l + k // 2 + 1)
                    a.activation(h32[:, k, :], bank[4 + k // 2][:, 256 * (k % 2):256 * (k % 2) + 256], ACT.Identity,
                                 scale=g2[:, k:k + 1]).then_inc(S("h32_act"), 1)
                for t in range(T):
                    if t == 0:
                        act.wait_ge(S("n2_xa"), l + 1)
                    else:
                        act.wait_ge(S("n2_xd"), l + 1)
                    a.activation(xt_hi[:, t, :, :], xn[:, t, :, :], ACT.Copy).then_inc(S("xt_hi_done"), 1)
                hi(at, 2)
                act.wait_ge(S("gd_done"), l + 1)
                a.activation(r4[:, 2, :, :].rearrange("p t g -> p (t g)"), r4[:, 1, :, :].rearrange("p t g -> p (t g)"),
                             ACT.Exp).then_inc(S("ge_done"), 1)
                for k in range(KT):
                    act.wait_ge(S("g_tp"), KT * l + k + 1)
                    a.activation(xg[:, k, :], bank[4 + k % 4][:, :], ACT.Identity,
                                 scale=g2[:, k:k + 1]).then_inc(S("g_act"), 1)
                    if k == 3:
                        act.wait_ge(S("dm_done"), l + 1)
                        a.activation(r1[:, 8, :], r1[:, 7, :], ACT.Exp).then_inc(S("x2_done"), 1)
                    if k == 5:
                        act.wait_ge(S("g_act"), KT * l + 4)
                        pass_tokens(0, 0)
                act.wait_ge(S("tab_ready"), l + 1)
                act.wait_ge(S("g_act"), KT * (l + 1))
                pass_tokens(1, 0)
                npass = act.value_load(tab[0:1, 0, 6:7], min_val=NG, max_val=NG + 1)
                with act.Fori(0, npass) as p:
                    tile = act.value_load(tab[0:1, 1, bass.ds(p + 1, 1)], min_val=0, max_val=NG - 1)
                    PP = before + p
                    at = At(l, PP, True)

                    def silu(e):
                        act.wait_ge(unit_used, at.unit((1, 3, 6, 9)[e]) + PART + 1)
                        a.activation(sil[:, e % 2, :], bank[6 + e % 2][:, 0:F], ACT.Silu).then_inc(S("sil_done"), 1)

                    def hidden(e):
                        act.wait_ge(S("hid_tp"), EPG * PP + e + 1)
                        a.activation(hd_hi[:, e % 2, :, :].rearrange("p f s -> p (f s)"), bank[6 + e % 2][:, 0:F],
                                     ACT.Copy).then_inc(S("hd_hi_done"), 1)

                    a.activation(warm[:, 0:1], ones[0:1, 0:1], ACT.Silu)
                    hi(at, 3)
                    hi(at, 4)
                    silu(0)
                    hi(at, 5)
                    hidden(0)
                    hi(at, 6)
                    silu(1)
                    hi(at, 7)
                    hi(at, 8)
                    hidden(1)
                    hi(at, 9)
                    silu(2)
                    hi(at, 10)
                    hi(at, 11)
                    hidden(2)
                    silu(3)
                    pass_tokens(0, tile * P)
                    pass_tokens(1, tile * P)
                    ahead = At(l, PP + 1, True)
                    hi(ahead, 0)
                    hidden(3)
                    hi(ahead, 1)
                    for h in range(2):
                        if h == 0:
                            act.wait_ge(S("y_bank"), PP + 1)
                        else:
                            used(at, 11)
                        a.activation(z_hi[:, 512 * h:512 * h + 512], bank[4 + h][:, :], ACT.Copy).then_inc(S("z_hi_done"), 1)
                    hi(ahead, 2)
                for t in range(T):
                    act.wait_ge(S("x_out"), 2 * T * l + 2 * t + 2)
                    square(t)
                scale_rows(l + 1, "n1", 0)

        @block.vector
        def _(dve):
            v = nc.vector
            step = Steps(dve, dve_step)

            def lo(at, n):
                slot, part = at.slot(n, RAW), at.slot(n, PART)
                dve.wait_ge(hi_done, at.unit(n) + 1)
                w = width(n, at.moe)
                v.tensor_tensor(w_lo[:, part, 0:w], raw[:, slot, 0:w], w_hi[:, part, 0:w].bitcast(F32),
                                ALU.subtract).then_inc(split_done, 1)

            def pass_low(passes, half, slot):
                dve.wait_ge(S("gp_hi"), 2 * passes + half + 1)
                k = slice(4 * half, 4 * half + 4)
                v.tensor_tensor(g_lo[:, k, :], xg[:, k, bass.ds(slot, P)], g_hi[:, k, :].bitcast(F32),
                                ALU.subtract).then_inc(S("gp_lo"), 1)

            def bc(ap, shape, axis):
                return ap.unsqueeze(axis).to_broadcast(shape)

            v.memset(dpad[:, :, 0:K31 - 1], 0.0).then_inc(split_done, RAW)
            v.memset(bx[:, 0, 0:K3 - 1], 0.0).then_inc(unit_used, PART)
            v.memset(bx[:, 1, 0:K3 - 1], 0.0)
            step.do(v.memset(tab_f[:, :, :], 0.0))
            v.tensor_copy(tab[:, :, :], tab_f[:, :, :]).then_inc(S("tab_zero"), 1)
            dve.wait_ge(pos_loaded, 16)
            ang = rope[:, 0, 0:2, 0:2, :]
            cyc = rope[:, 1, 0:2, 0:2, :]
            posf = v_mu
            step.do(v.tensor_copy(posf[:, :], posi[:, :]))
            inv = [float(np.float32(ROPE_THETA ** (-2.0 * j / ROT))) for j in range(HALF)]
            for j in range(HALF):
                step.do(v.tensor_scalar(ang[:, 1, :, j], posf[:, :], inv[j], None, ALU.mult))
            step.do(v.tensor_scalar(cyc[:, 1], ang[:, 1], float(np.float32(1 / (2 * np.pi))), None, ALU.mult))
            step.do(v.tensor_scalar(cyc[:, 0], cyc[:, 1], 0.25, None, ALU.add))
            big = float(1.5 * 2 ** 23)
            step.do(v.tensor_scalar(cyc, cyc, big, None, ALU.add))
            step.do(v.tensor_scalar(cyc, cyc, big, None, ALU.subtract))
            step.do(v.tensor_copy(ang[:, 0], ang[:, 1]))
            c1 = 6.28125
            c2 = float(np.float32(np.floor((2 * np.pi - c1) * 2 ** 20) / 2 ** 20))
            c3 = float(np.float32(2 * np.pi - c1 - c2))
            for c in (c1, c2, c3):
                step.do(v.scalar_tensor_tensor(out=ang, in0=cyc, scalar=-c, in1=ang, op0=ALU.mult, op1=ALU.add))
            step.do(v.tensor_scalar(ang[:, 0], ang[:, 0], float(np.float32(np.pi / 2)), None, ALU.add))
            pi = float(np.float32(3.1415925))
            v.tensor_scalar(ang, ang, pi, -pi, ALU.min, ALU.max).then_inc(S("angles"), 1)
            dve.wait_ge(pool_consts, 14)
            for i in range(3):
                step.do(v.tensor_copy(tab_f[:, i, 0:NG], widx[:, 1, :]))
            n_first = step.n

            def rstd_input(l, n):
                dve.wait_ge(S(n + "_ssq"), T * (l + 1))
                v.tensor_scalar(ssq[:, :], ssq[:, :], 1.0 / D, EPS, ALU.mult, ALU.add).then_inc(S(n + "_ms"), 1)

            def scale_rows(l, n, t):
                dve.wait_ge(S(n + "_rs"), l + 1)
                v.tensor_scalar(xn[:, t, :, :], x[:, t, :].rearrange("q (p c) -> q c p", c=KT), rstd[:, t:t + 1], None,
                                ALU.mult).then_inc(S(n + "_xd"), 1)

            rstd_input(0, "n1")
            scale_rows(0, "n1", 1)
            for n in range(AHEAD):
                lo(At(0, 0, False), n)
                if n < 2:
                    dve.wait_ge(pool_consts, 25 + 3 * n)
                    v.tensor_copy(bsel[:, 4 * n:4 * n + 4, :].rearrange("p b s -> p (b s)"),
                                  bsel_f[0:16, 0:512]).then_inc(S("bsel_copied"), 1)
            with dve.Fori(0, DEPTH) as l:
                before = dve.value_load(tab[0:1, 0, 7:8], min_val=0, max_val=DEPTH * (NG + 1))
                step.at(n_first + DVE_STEPS * l)
                at = At(l, before, False)
                for k in range(KT):
                    dve.wait_ge(S("h_hi_done"), KT * l + 2 * (k // 2) + 2)
                    v.scalar_tensor_tensor(out=h_lo[:, k, :], in0=bank[4 + k // 2][:, 256 * (k % 2):256 * (k % 2) + 256],
                                           scalar=g1[:, k:k + 1], in1=h_hi[:, k, :].bitcast(F32),
                                           op0=ALU.mult, op1=ALU.subtract).then_inc(S("h_lo_done"), 1)
                dve.wait_ge(S("bg_hi_done"), l + 1)
                step.do(v.tensor_scalar(bg_raw[:, :], bg_raw[:, :], s12[:, 1:2], None, ALU.mult))
                v.scalar_tensor_tensor(out=bg[:, :], in0=bg_hi[:, :].bitcast(F32), scalar=s12[:, 0:1], in1=bg_raw[:, :],
                                       op0=ALU.mult, op1=ALU.add).then_inc(S("bg_done"), 1)
                dve.wait_ge(S("sgw_tp"), l + 1)
                v.tensor_tensor(sgw_t[:, :, :], bank[4][:, :].rearrange("p (g t) -> p g t", g=GS),
                                bc(upto[:, :], [P, GS, P], 1), ALU.mult).then_inc(S("sgw_done"), 1)
                dve.wait_ge(S("cols_tp"), l + 1)
                v.tensor_copy(cols[:, :, :], bank[5][:, 0:CT * NROW].rearrange("p (c r) -> p c r", c=CT)).then_inc(S("cols_done"), 1)
                lo(at, 3)
                lo(at, 4)
                lo(at, 5)
                dve.wait_ge(S("win_act"), 7 * l + 2)
                step.do(v.tensor_scalar(v_mu[:, :], v_mu[:, :], -1.0 / MIX, None, ALU.mult))
                for t in range(T):
                    step.do(v.tensor_scalar(v_n[:, t, :], v_n[:, t, :], v_mu[:, t:t + 1], None, ALU.add))
                v_sq = y_tmp[:, :].rearrange("p (t c) -> p t c", t=T)
                step.do(v.tensor_tensor(v_sq, v_n[:, :, :], v_n[:, :, :], ALU.mult))
                step.do(v.tensor_reduce(v_ss[:, :], v_sq, AX, ALU.add))
                v.tensor_scalar(v_ss[:, :], v_ss[:, :], 1.0 / MIX, EPS, ALU.mult, ALU.add).then_inc(S("v_ms"), 1)
                lo(at, 6)
                dve.wait_ge(S("v_rs_done"), l + 1)
                for t in range(T):
                    step.do(v.scalar_tensor_tensor(out=v_n[:, t, :], in0=v_n[:, t, :], scalar=v_rs[:, t:t + 1],
                                                   in1=lng[:, :], op0=ALU.mult, op1=ALU.mult))
                v.tensor_tensor(v_n[:, :, :], v_n[:, :, :], bc(lnb[:, :], [P, T, MIX], 1), ALU.add).then_inc(S("vn_done"), 1)
                lo(at, 7)
                dve.wait_ge(S("win_act"), 7 * l + 4)
                qkin = qkv[:, :, 0:NH * HD].rearrange("p t (h d) -> p t h d", h=NH)
                step.do(v.tensor_tensor(qk[:, :, :, :], qkin, qkin, ALU.mult))
                step.do(v.tensor_reduce(qkss[:, :], qk[:, :, :, :].rearrange("p t h d -> p (t h) d"), AX, ALU.add))
                v.tensor_scalar(qkss[:, :], qkss[:, :], 1.0 / HD, EPS, ALU.mult, ALU.add).then_inc(S("qk_ms"), 1)
                lo(at, 8)
                lo(at, 9)
                lo(at, 10)
                dve.wait_ge(S("rope_ready"), 1)
                dve.wait_ge(S("qk_rs"), l + 1)
                rs = qkrs[:, :].rearrange("p (t h) -> p t h", t=T)
                for t in range(T):
                    step.do(v.tensor_tensor(qk[:, t, 0:NQ, :].rearrange("p (b a) d -> p a b d", a=2),
                                            qkin[:, t, 0:NQ, :].rearrange("p (a b) d -> p a b d", a=2),
                                            bc(rs[:, t, 0:NQ].rearrange("p (a b) -> p a b", a=2), [P, 2, 2, HD], 3),
                                            ALU.mult))
                    step.do(v.tensor_tensor(qk[:, t, NQ:NH, :], qkin[:, t, NQ:NH, :],
                                            bc(rs[:, t, NQ:NH], [P, NKV, HD], 2), ALU.mult))
                for t in range(T):
                    step.do(v.tensor_tensor(qk[:, t, 0:NQ, :], qk[:, t, 0:NQ, :], bc(qg[:, :], [P, NQ, HD], 1), ALU.mult))
                    step.do(v.tensor_tensor(qk[:, t, NQ:NH, :], qk[:, t, NQ:NH, :], bc(kg[:, :], [P, NKV, HD], 1),
                                            ALU.mult))
                x1, x2 = qk[:, :, :, 0:HALF], qk[:, :, :, HALF:ROT]
                cs, sn = (bc(cos_sin[:, i, :, :], [P, T, NH, HALF], 2) for i in range(2))
                for i, (aa, bb) in enumerate(((x1, cs), (x2, sn), (x2, cs), (x1, sn))):
                    step.do(v.tensor_tensor(rope[:, i], aa, bb, ALU.mult))
                step.do(v.tensor_tensor(x1, rope[:, 0], rope[:, 1], ALU.subtract))
                v.tensor_tensor(x2, rope[:, 2], rope[:, 3], ALU.add).then_inc(S("qk_done"), 1)
                lo(at, 11)
                used = lambda n: dve.wait_ge(unit_used, at.unit(n) + PART + 1)
                used(7)
                dve.wait_ge(S("win_act"), 7 * l + 6)
                v.tensor_tensor(bx[:, :, K3 - 1:], bank[2][:, :].rearrange("p (c s) -> p c s", c=CT), c_b[:, :, :],
                                ALU.mult).then_inc(S("win_dve"), 1)
                lo(at, 12)
                lo(at, 13)
                dve.wait_ge(S("win_act"), 7 * l + 7)
                v.tensor_tensor(dpad[:, :, K31 - 1:], bank[3][:, :].rearrange("p (c s) -> p c s", c=CT), d_sig[:, :, :],
                                ALU.mult).then_inc(S("win_dve"), 1)
                dve.wait_ge(S("win_dve"), 2 * (l + 1))
                lo(at, 14)
                dve.wait_ge(S("cols_done"), l + 1)
                yc = c_b
                for k in range(K3):
                    for c in range(CT):
                        w = cols[:, c, K31 + 3 + k:K31 + 4 + k]
                        src = bx[:, c, k:k + SEQ]
                        if k == 0:
                            last = v.tensor_scalar(yc[:, c, :], src, w, None, ALU.mult)
                        else:
                            last = v.scalar_tensor_tensor(out=yc[:, c, :], in0=src, scalar=w, in1=yc[:, c, :],
                                                          op0=ALU.mult, op1=ALU.add)
                        last.then_inc(dve_step, 1)
                        step.n += 1
                        if c == 1:
                            step.upto(step.n)
                v.tensor_tensor(yc_out, yc[:, :, :].rearrange("p c s -> p (c s)"),
                                c_gate[:, :, :].rearrange("p c s -> p (c s)"), ALU.mult).then_inc(S("yc_done"), 1)

                def taps(k0, k1):
                    for k in range(k0, k1):
                        for c in range(CT):
                            w = cols[:, c, k:k + 1]
                            src = dpad[:, c, k:k + SEQ]
                            if k == 0:
                                last = v.tensor_scalar(d_acc[:, c, :], src, w, cols[:, c, K31:K31 + 1], ALU.mult, ALU.add)
                            else:
                                step.upto(step.n - 1)
                                last = v.scalar_tensor_tensor(out=d_acc[:, c, :], in0=src, scalar=w,
                                                              in1=d_acc[:, c, :], op0=ALU.mult, op1=ALU.add)
                            last.then_inc(dve_step, 1)
                            step.n += 1

                lo(at, 15)
                own = bc(amask[:, P:2 * P], [P, NQ, P], 1)
                dve.wait_ge(S("sc_tp"), 3 * l + 1)
                step.do(v.scalar_tensor_tensor(out=sc[0], in0=bank[4][:, :].rearrange("p (h k) -> p h k", h=NQ),
                                               scalar=HD ** -0.5, in1=own, op0=ALU.mult, op1=ALU.add))
                for i in range(2):
                    dve.wait_ge(S("sc_tp"), 3 * l + 2 + i)
                    step.do(v.scalar_tensor_tensor(out=sc[1][:, 2 * i:2 * i + 2, :],
                                                   in0=bank[5 + i][:, :].rearrange("p (h k) -> p h k", h=2),
                                                   scalar=HD ** -0.5, in1=bc(amask[:, :], [P, 2, 2 * P], 1),
                                                   op0=ALU.mult, op1=ALU.add))
                for t in range(T):
                    step.do(v.tensor_reduce(st[:, 0, t, :], sc[t], AX, ALU.max))
                step.do(v.tensor_tensor(st[:, 0, :, :], st[:, 0, :, :], bc(snk[:, :], [P, T, NQ], 1), ALU.max))
                step.do(v.tensor_tensor(st[:, 3, :, :], bc(snk[:, :], [P, T, NQ], 1), st[:, 0, :, :], ALU.subtract))
                v.tensor_scalar(st[:, 1, :, :], st[:, 0, :, :], -1.0, None, ALU.mult).then_inc(S("mx_done"), 1)
                lo(at, 16)
                lo(at, 17)
                dve.wait_ge(S("z_done"), l + 1)
                v.tensor_tensor(u_t[:, :], bank[7][:, :], u_t[:, :], ALU.mult).then_inc(S("ya_done"), 1)
                taps(0, 4)
                dve.wait_ge(S("exp_done"), 9 * (l + 1))
                step.do(v.tensor_tensor(st[:, 2, :, :], st[:, 2, :, :], st[:, 4, :, :], ALU.add))
                step.do(v.reciprocal(st[:, 5, :, :], st[:, 2, :, :]))
                for t in range(T):
                    v.tensor_tensor(sc[t], sc[t], bc(st[:, 5, t, :], [P, NQ, (t + 1) * P], 2), ALU.mult).then_inc(S("p_done"), 1)
                lo(at, 18)
                taps(4, 9)
                lo(at, 19)
                taps(9, 14)
                lo(at, 20)
                taps(14, 19)
                lo(at, 21)
                taps(19, 24)
                lo(at, 22)
                for i, (src, n) in enumerate(((u_t[:, :], 0), (yc_out, 2))):
                    dve.wait_ge(S("y_hi_done"), 4 * l + i + 1)
                    v.tensor_tensor(y_lo[:, n, :], src, y_hi[:, n, :].bitcast(F32), ALU.subtract).then_inc(S("y_lo_done"), 1)
                taps(24, 28)
                lo(at, 23)
                taps(28, K31)
                dve.wait_ge(S("y_hi_done"), 4 * l + 3)
                v.tensor_tensor(y_lo[:, 1, :], bank[6][:, :], y_hi[:, 1, :].bitcast(F32), ALU.subtract).then_inc(S("y_lo_done"), 1)
                lo(at, 24)
                step.upto(step.n)
                v.tensor_copy(c_b[:, 0, 0:1], d_acc[:, 0, 0:1]).then_inc(S("conv_done"), 1)
                lo(at, 25)
                lo(at, 26)
                dve.wait_ge(S("dsum_done"), l + 1)
                v.scalar_tensor_tensor(out=d_acc[:, :, :], in0=bc(bank[4][:, 0:SEQ], [P, CT, SEQ], 1), scalar=-1.0 / MIX,
                                       in1=d_acc[:, :, :], op0=ALU.mult, op1=ALU.add).then_inc(S("dc_done"), 1)
                lo(at, 27)
                lo(at, 28)
                dve.wait_ge(S("dvar_done"), l + 1)
                v.tensor_scalar(dn[0], bank[5][:, 0:SEQ], 1.0 / MIX, EPS, ALU.mult, ALU.add).then_inc(S("dv_done"), 1)
                lo(at, 29)
                dve.wait_ge(S("dr0_done"), l + 1)
                step.do(v.tensor_tensor(dn[2], dn[1], dn[1], ALU.mult))
                step.do(v.tensor_tensor(dn[2], dn[2], dn[0], ALU.mult))
                step.do(v.tensor_scalar(dn[2], dn[2], -0.5, 1.5, ALU.mult, ALU.add))
                step.do(v.tensor_tensor(dn[1], dn[1], dn[2], ALU.mult))
                v.tensor_tensor(d_acc[:, :, :], d_acc[:, :, :], bc(dn[1], [P, CT, SEQ], 1), ALU.mult).then_inc(S("dx_done"), 1)

                def conformer_low():
                    dve.wait_ge(S("y_hi_done"), 4 * (l + 1))
                    v.tensor_tensor(y_lo[:, 3, :], d_sig[:, :, :].rearrange("p c s -> p (c s)"),
                                    y_hi[:, 3, :].bitcast(F32), ALU.subtract).then_inc(S("y_lo_done"), 1)

                def merged_low(q):
                    dve.wait_ge(S("m_hi_done"), 4 * l + q + 1)
                    v.tensor_tensor(merged_part(h_lo, q), bank[q][:, :].rearrange("p (k s) -> p k s", k=4),
                                    merged_part(h_hi, q).bitcast(F32), ALU.subtract).then_inc(S("m_lo_done"), 1)

                def merge(n):
                    dve.wait_ge(S("gates_done"), 16 * l + 4 * n + 4)

                    def add(i):
                        t, h = i // 2, i % 2
                        dst = merged[:, t, 512 * h:512 * h + 512]
                        dve.wait_ge(S("y_evac"), 16 * l + 4 * n + i + 1)
                        if n > 1:
                            dve.wait_ge(S("m_add"), 12 * l + 4 * (n - 2) + i + 1)
                        v.tensor_tensor(dst, dst, gates[:, 2 * n + h, t, :], ALU.add).then_inc(S("m_add"), 1)

                    for i in range(4):
                        t, h = i // 2, i % 2
                        if i < 3:
                            dve.wait_ge(S("y_job"), 12 * l + 3 * n + i + 1)
                        else:
                            used(Y0 + n)
                        gt = gates[:, 2 * n + h, t, :]
                        dst = merged[:, t, 512 * h:512 * h + 512] if n == 0 else gt
                        v.tensor_tensor(dst, bank[4 * (n % 2) + i][:, :], gt, ALU.mult).then_inc(S("y_evac"), 1)
                        if n == NBR - 1:
                            add(i)
                            if i == 2:
                                merged_low(0)
                                merged_low(1)
                                lo(at, 31)
                    if 0 < n < NBR - 1:
                        for i in range(4):
                            add(i)

                merge(0)
                conformer_low()
                lo(at, 30)
                merge(1)
                merge(2)
                merge(3)
                merged_low(2)
                merged_low(3)
                for n in range(32, NA):
                    lo(at, n)
                at_m = At(l, before, True)
                lo(at_m, 0)
                for i in range(4):
                    if i == 0:
                        dve.wait_ge(S("o_half"), l + 1)
                    elif i == 2:
                        used(NA - 1)
                    xs = x[:, i // 2, 512 * (i % 2):512 * (i % 2) + 512]
                    v.tensor_tensor(xs, bank[4 + i][:, :], xs, ALU.add).then_inc(S("x_mid"), 1)

                at = at_m
                rstd_input(l, "n2")
                scale_rows(l, "n2", 1)
                lo(at, 1)
                dve.wait_ge(par_r, 16 * 5 * (l + 1))
                for k in (2, 3, 6, 7):
                    dve.wait_ge(S("n2_t"), 4 * l + k // 2 + 1)
                    v.tensor_scalar(h32[:, k, :], bank[4 + k // 2][:, 256 * (k % 2):256 * (k % 2) + 256], g2[:, k:k + 1], None,
                                    ALU.mult).then_inc(S("h32_dve"), 1)
                for t in range(T):
                    dve.wait_ge(S("xt_hi_done"), T * l + t + 1)
                    v.tensor_tensor(xt_lo[:, t, :, :], xn[:, t, :, :], xt_hi[:, t, :, :].bitcast(F32),
                                    ALU.subtract).then_inc(S("xt_lo_done"), 1)
                lo(at, 2)
                dve.wait_ge(S("lt_done"), l + 1)
                v.tensor_scalar(lt[:, :], bank[0][0:NR, 0:SEQ], rb[:, 0:1], None, ALU.add).then_inc(S("lt_sb"), 1)
                dve.wait_ge(S("lg_tp"), l + 1)
                step.do(v.tensor_copy(lg[:, :, :], bank[1][:, 0:T * NR].rearrange("p (t r) -> p t r", t=T)))
                gl = lg[:, :, 0:NG]
                el = lg[:, :, NG:NR].rearrange("p t (g e) -> p t g e", g=NG)
                b4 = lambda ap: bc(ap, [P, T, NG], 2)
                wi = lambda i: bc(widx[:, i, :], [P, T, NG], 1)

                def first_max(dst, val, m, i):
                    step.do(v.tensor_reduce(m, val, AX, ALU.max))
                    step.do(v.tensor_tensor(dst, val, b4(m), ALU.is_equal))
                    step.do(v.tensor_tensor(dst, dst, wi(0), ALU.mult))
                    step.do(v.tensor_reduce(r1[:, i, :], dst, AX, ALU.max))
                    step.do(v.tensor_tensor(dst, dst, b4(r1[:, i, :]), ALU.is_equal))

                goh, gm = r4[:, 0], r1[:, 0]
                first_max(goh, gl, gm, 1)
                v.tensor_copy(r4[:, 3], goh).then_inc(S("goh_done"), 1)
                v.tensor_tensor(r4[:, 1], gl, b4(gm), ALU.subtract).then_inc(S("gd_done"), 1)
                for i, w in ((12, 1), (13, 2)):
                    step.do(v.tensor_tensor(r4[:, 8], goh, wi(w), ALU.mult))
                    step.do(v.tensor_reduce(r1[:, i, :], r4[:, 8], AX, ALU.add))
                dve.wait_ge(S("rank_done"), l + 1)
                step.do(v.tensor_tensor(r4[:, 8], bank[2][:, 0:T * NG].rearrange("p (t g) -> p t g", t=T), goh, ALU.mult))
                step.do(v.tensor_reduce(r1[:, 11, :], r4[:, 8], AX, ALU.add))
                step.do(v.tensor_copy(cnt[:, 0, :], bank[2][:, T * NG:T * NG + NG]))
                rk, ov = r1[:, 11, :], r1[:, 14, :]
                step.do(v.tensor_scalar(ov, rk, float(P), None, ALU.is_ge))
                step.do(v.scalar_tensor_tensor(out=r1[:, 15, :], in0=r1[:, 12, :], scalar=float(P), in1=rk,
                                               op0=ALU.mult, op1=ALU.add))
                step.do(v.scalar_tensor_tensor(out=r1[:, 16, :], in0=r1[:, 13, :], scalar=float(P), in1=rk,
                                               op0=ALU.mult, op1=ALU.subtract))
                step.do(v.scalar_tensor_tensor(out=r1[:, 16, :], in0=r1[:, 16, :], scalar=float(2 * P - 1),
                                               in1=r1[:, 15, :], op0=ALU.add, op1=ALU.subtract))
                step.do(v.tensor_tensor(r1[:, 16, :], r1[:, 16, :], ov, ALU.mult))
                pos = r1[:, 17, :]
                step.do(v.tensor_tensor(pos, r1[:, 15, :], r1[:, 16, :], ALU.add))
                for t in range(T):
                    v.tensor_scalar(sel[:, t, :], iota[:, :], r1[:, 17, t:t + 1], None, ALU.is_equal).then_inc(S("sel_done"), 1)
                for t in range(T):
                    v.tensor_scalar(diag[:, t, :], ident[:, :], r1[:, 17, t:t + 1], None, ALU.mult).then_inc(S("diag_done"), 1)
                step.do(v.tensor_tensor(pr, el, bc(goh, [P, T, NG, EPG], 3), ALU.mult))
                ein, oh1, e2, oh2 = r4[:, 4], r4[:, 5], r4[:, 6], r4[:, 7]
                step.do(v.tensor_reduce(ein, pr.rearrange("p t g e -> p t e g"), AX, ALU.add))
                first_max(oh1, ein, r1[:, 3], 4)
                step.do(v.scalar_tensor_tensor(out=e2, in0=oh1, scalar=NEG, in1=ein, op0=ALU.mult, op1=ALU.add))
                first_max(oh2, e2, r1[:, 5], 6)
                v.tensor_tensor(r1[:, 7, :], r1[:, 5, :], r1[:, 3, :], ALU.subtract).then_inc(S("dm_done"), 1)
                dve.wait_ge(S("ge_done"), l + 1)
                step.do(v.tensor_reduce(r1[:, 9, :], r4[:, 2], AX, ALU.add))
                step.do(v.reciprocal(r1[:, 10, :], r1[:, 9, :]))
                step.do(v.tensor_scalar(cnt[:, 1, :], cnt[:, 0, :], float(P), None, ALU.is_gt))
                step.do(v.tensor_tensor(cnt[:, 2, :], cnt[:, 1, :], widx[:, 1, :], ALU.mult))
                step.do(v.tensor_tensor(cnt[:, 3, :], cnt[:, 1, :], widx[:, 2, :], ALU.mult))
                step.do(v.tensor_reduce(tab_f[:, 0, NG:NG + 1], cnt[:, 2, :], AX, ALU.add))
                step.do(v.tensor_reduce(tab_f[:, 1, NG:NG + 1], cnt[:, 3, :], AX, ALU.add))
                step.do(v.tensor_scalar(tab_f[:, 2, NG:NG + 1], tab_f[:, 1, NG:NG + 1], float(NG), None, ALU.add))
                step.do(v.tensor_reduce(tab_f[:, 0, 6:7], cnt[:, 1, :], AX, ALU.add))
                step.do(v.tensor_scalar(tab_f[:, 0, 6:7], tab_f[:, 0, 6:7], float(NG), None, ALU.add))
                step.do(v.tensor_tensor(tab_f[:, 0, 7:8], tab_f[:, 0, 7:8], tab_f[:, 0, 6:7], ALU.add))
                v.tensor_copy(tab[:, :, :], tab_f[:, :, :]).then_inc(S("tab_ready"), 1)
                dve.wait_ge(S("posb_done"), l + 1)
                v.tensor_copy(posb[:, :], bank[3][:, 0:SEQ]).then_inc(S("posb_read"), 1)
                dve.wait_ge(S("x2_done"), l + 1)
                step.do(v.tensor_scalar(r1[:, 18, :], r1[:, 8, :], 1.0, None, ALU.add))
                step.do(v.reciprocal(r1[:, 19, :], r1[:, 18, :]))
                step.do(v.tensor_tensor(r1[:, 20, :], r1[:, 19, :], r1[:, 8, :], ALU.mult))
                step.do(v.tensor_tensor(r1[:, 19, :], r1[:, 19, :], r1[:, 10, :], ALU.mult))
                step.do(v.tensor_tensor(r1[:, 20, :], r1[:, 20, :], r1[:, 10, :], ALU.mult))
                step.do(v.tensor_tensor(r4[:, 9], oh1, b4(r1[:, 19, :]), ALU.mult))
                step.do(v.tensor_tensor(r4[:, 10], oh2, b4(r1[:, 20, :]), ALU.mult))
                step.do(v.tensor_tensor(r4[:, 9], r4[:, 9], r4[:, 10], ALU.add))
                step.do(v.tensor_tensor(cmf[:, :, 4:8], r4[:, 9], b4(ov), ALU.mult))
                v.tensor_tensor(cmf[:, :, 0:4], r4[:, 9], cmf[:, :, 4:8], ALU.subtract).then_inc(S("cmf_done"), 1)
                dve.wait_ge(S("cmf_done"), l + 1)
                v.tensor_copy(cmr[:, :, 0:8], cmf[:, :, :]).then_inc(S("cm_hi_done"), 1)
                dve.wait_ge(S("cm_hi_done"), l + 1)
                v.tensor_tensor(cmr[:, :, 8:16], cmf[:, :, :], cmr[:, :, 0:8].bitcast(F32), ALU.subtract).then_inc(S("cm_lo_done"), 1)
                pass_low(before + l, 0, 0)
                pass_low(before + l, 1, 0)
                dve.wait_ge(S("cw_done"), l + 1)
                step.do(v.tensor_copy(cwf[:, :, :], bank[4][:, 0:NG * 16].rearrange("p (g n) -> p g n", g=NG)))
                v.tensor_tensor(cwt[:, :, :].rearrange("p (m g) e -> p g m e", m=2),
                                cwf[:, :, 0:8].rearrange("p g (m e) -> p g m e", m=2),
                                cwf[:, :, 8:16].rearrange("p g (m e) -> p g m e", m=2), ALU.add).then_inc(S("cw_read"), 1)
                assert step.n == DVE_STEPS, ("dve steps of a layer", step.n)

                dve.wait_ge(S("cw_read"), l + 1)
                dve.wait_ge(S("tab_ready"), l + 1)
                v.memset(sel_t.bitcast(F32), 0.0).then_inc(S("selt_done"), 1)
                npass = dve.value_load(tab[0:1, 0, 6:7], min_val=NG, max_val=NG + 1)
                with dve.Fori(0, npass) as p:
                    tile = dve.value_load(tab[0:1, 1, bass.ds(p, 1)], min_val=0, max_val=NG - 1)
                    tile_next = dve.value_load(tab[0:1, 1, bass.ds(p + 1, 1)], min_val=0, max_val=NG - 1)
                    cw = dve.value_load(tab[0:1, 2, bass.ds(p, 1)], min_val=0, max_val=2 * NG - 1)
                    PP = before + p
                    at = At(l, PP, True)
                    cwf2 = cwt.rearrange("p q e -> p (q e)")

                    def hidden(e):
                        dve.wait_ge(S("sil_done"), EPG * PP + e + 1)
                        v.scalar_tensor_tensor(out=hid[:, e % 2, :], in0=sil[:, e % 2, :],
                                               scalar=cwf2[:, bass.ds(cw * EPG + e, 1)], in1=bank[6 + e % 2][:, F:2 * F],
                                               op0=ALU.mult, op1=ALU.mult).then_inc(S("hid_done"), 1)

                    def hidden_lo(e):
                        dve.wait_ge(S("hd_hi_done"), EPG * PP + e + 1)
                        v.tensor_tensor(hd_lo[:, e % 2, :, :].rearrange("p f s -> p (f s)"), bank[6 + e % 2][:, 0:F],
                                        hd_hi[:, e % 2, :, :].rearrange("p f s -> p (f s)").bitcast(F32),
                                        ALU.subtract).then_inc(S("hd_lo_done"), 1)

                    lo(at, 3)
                    hidden(0)
                    lo(at, 4)
                    hidden_lo(0)
                    lo(at, 5)
                    hidden(1)
                    lo(at, 6)
                    lo(at, 7)
                    hidden_lo(1)
                    lo(at, 8)
                    hidden(2)
                    lo(at, 9)
                    lo(at, 10)
                    hidden_lo(2)
                    lo(at, 11)
                    hidden(3)
                    pass_low(PP + l + 1, 0, tile_next * P)
                    pass_low(PP + l + 1, 1, tile_next * P)
                    hidden_lo(3)
                    ahead = At(l, PP + 1, True)
                    lo(ahead, 0)
                    lo(ahead, 1)
                    dve.wait_ge(S("scattered"), PP + l + 1)
                    v.tensor_scalar(sel_t, posb[:, :], icol[:, bass.ds(tile, 1)], None, ALU.is_equal)
                    for h in range(2):
                        dve.wait_ge(S("z_hi_done"), 2 * PP + h + 1)
                        last = v.tensor_tensor(z_lo[:, 512 * h:512 * h + 512], bank[4 + h][:, :],
                                               z_hi[:, 512 * h:512 * h + 512].bitcast(F32), ALU.subtract)
                    last.then_inc(S("selt_done"), 1)
                    lo(ahead, 2)
                dve.wait_ge(S("scattered"), before + npass + l + 1)
                for i in range(4):
                    xs = x[:, i // 2, 512 * (i % 2):512 * (i % 2) + 512]
                    v.tensor_tensor(xs, bank[i][:, :], xs, ALU.add).then_inc(S("x_out"), 1)
                rstd_input(l + 1, "n1")
                scale_rows(l + 1, "n1", 1)

        @block.tensor
        def _(pe):
            mm = nc.tensor.matmul
            tp = nc.tensor.transpose

            def ready(at, n):
                pe.wait_ge(split_done, at.unit(n) + RAW + 1)

            def three(ps, a2, b2, first, last, shared=False):
                mm(ps, a2[0], b2[0], start=first, stop=False, skip_group_check=shared)
                mm(ps, a2[1], b2[0], start=False, stop=False, skip_group_check=shared)
                return mm(ps, a2[0], b2[1], start=False, stop=last, skip_group_check=shared)

            def parts(at, n, shape, **kw):
                s = at.slot(n, PART)
                return [w[:, s, :].rearrange(shape, **kw) for w in (w_hi, w_lo)]

            def both(pair, *ix):
                return [w[(slice(None),) + ix] for w in pair]

            H = [h_hi, h_lo]
            pe.wait_ge(pool_consts, 25)
            pe.wait_ge(S("tab_zero"), 1)
            with pe.Fori(0, DEPTH) as l:
                before = pe.value_load(tab[0:1, 0, 7:8], min_val=0, max_val=DEPTH * (NG + 1))
                at = At(l, before, False)
                pe.wait_ge(S("n1_xa"), l + 1)
                pe.wait_ge(S("n1_xd"), l + 1)
                for k in range(KT):
                    for t in range(T):
                        c = 256 * (k % 2) + P * t
                        last = tp(bank[4 + k // 2][:, c:c + P], xn[:, t, k, :], ident[:, :])
                    if k % 2:
                        last.then_inc(S("n1_t"), 1)
                pe.wait_ge(S("h_lo_done"), KT * l + 4)
                pe.wait_ge(par_a, 16 * 14 * (l + 1))
                for g in range(GS):
                    last = tp(bank[4][:, P * g:P * g + P], sgw[:, g, :], ident[:, :])
                last.then_inc(S("sgw_tp"), 1)
                for c in range(CT):
                    last = tp(bank[5][:, NROW * c:NROW * c + NROW], rows[:, P * c:P * c + P], ident[0:NROW, 0:NROW])
                last.then_inc(S("cols_tp"), 1)

                def tokens(job, b2, k, t, first, last, col=0, n=512, shared=False):
                    return three(bank[job][:, col:col + n], both(H, k, slice(P * t, P * t + P)), b2, first, last, shared)

                def channels(job, wp, k, kk, f, first, last):
                    fb = f % 2
                    return three(bank[job][:, 256 * fb:256 * fb + 256], both(wp, kk, slice(P * f, P * f + P)),
                                 both(H, k), first and fb == 0, last, True)

                for b in range(4):
                    for h in range(2):
                        n = 2 * b + h
                        if h == 0 and b >= 2:
                            pe.wait_ge(S("win_act"), 7 * l + 2 * (b - 1))
                        if n == 1:
                            pe.wait_ge(S("h_lo_done"), KT * (l + 1))
                        ready(at, n)
                        wp = parts(at, n, "p (c m) -> p c m", c=4)
                        for kk in range(4):
                            k = 4 * h + kk
                            fi, la = k == 0, k == KT - 1
                            if b == 0:
                                for f in range(2):
                                    channels(0, wp, k, kk, f, fi, la)
                                for t in range(T):
                                    last = tokens(1, both(wp, kk, slice(256, 512)), k, t, fi and t == 0, la,
                                                  256 * t, 256, True)
                            elif b == 1:
                                for t in range(T):
                                    last = tokens(2 + t, both(wp, kk), k, t, fi, la)
                            else:
                                for f in range(4):
                                    last = channels(2 * (b % 2) + f // 2, wp, k, kk, f, fi, la)
                        last.then_inc(unit_used, 1)
                pe.wait_ge(S("win_act"), 7 * l + 5)
                for h in range(2):
                    ready(at, 8 + h)
                    wp = [w[:, 0:4, :] for w in parts(at, 8 + h, "p (c m) -> p c m", c=8)]
                    for kk in range(4):
                        for f in range(2):
                            last = channels(0, wp, 4 * h + kk, kk, f, h == 0 and kk == 0, 4 * h + kk == KT - 1)
                    last.then_inc(unit_used, 1)

                pe.wait_ge(S("bg_done"), l + 1)

                def gate_block(b):
                    for t in range(T):
                        if b == 0 and t == 0:
                            pe.wait_ge(S("win_act"), 7 * l + 6)
                        elif b == 0:
                            pe.wait_ge(S("win_dve"), 2 * l + 1)
                        elif b == 1 and t == 0:
                            pe.wait_ge(S("win_dve"), 2 * l + 2)
                        elif b == 1:
                            pe.wait_ge(S("win_act"), 7 * l + 7)
                        else:
                            pe.wait_ge(S("gates_done"), 16 * l + 2 * (b - 2) + t + 1)
                        mm(bank[(2 * b + t + 1) % 4][:, :], bsel[:, b, :], bg[:, :], start=True, stop=False)
                    for h in range(2):
                        n = G0 + 2 * b + h
                        ready(at, n)
                        wp = parts(at, n, "p (c m) -> p c m", c=4)
                        for kk in range(4):
                            for t in range(T):
                                last = tokens((2 * b + t + 1) % 4, both(wp, kk), 4 * h + kk, t, False,
                                              4 * h + kk == KT - 1)
                        last.then_inc(unit_used, 1)

                gate_block(0)
                pe.wait_ge(S("qk_done"), l + 1)
                for t in range(T):
                    for i in range(NH // 2):
                        last = tp(bank[6 + t][:, P * i:P * i + P],
                                  qk[:, t, 2 * i:2 * i + 2, :].rearrange("p h d -> p (h d)"), ident[:, :])
                    last.then_inc(S("qk_tp"), 1)
                gate_block(1)
                pe.wait_ge(S("qk_t_done"), T * (l + 1))

                def score(ps, h, tq, tk):
                    r = slice(HD * (h // 2), HD * (h // 2) + HD)
                    return mm(ps, qk_t[r, tq, P * (h % 2):P * (h % 2) + P], qk_t[r, tk, 2 * P:3 * P], start=True, stop=True)

                pe.wait_ge(S("sgw_done"), l + 1)
                pe.wait_ge(S("cols_done"), l + 1)
                for h in range(NQ):
                    last = score(bank[4][:, P * h:P * h + P], h, 0, 0)
                    if h == 1:
                        last.then_inc(S("sc_half"), 1)
                        pe.wait_ge(S("sc_half"), l + 1)
                last.then_inc(S("sc_tp"), 1)
                for i in range(2):
                    for h in (2 * i, 2 * i + 1):
                        for tk in range(T):
                            c = 256 * (h % 2) + P * tk
                            last = score(bank[5 + i][:, c:c + P], h, 1, tk)
                    last.then_inc(S("sc_tp"), 1)
                pe.wait_ge(S("vn_done"), l + 1)
                for c in range(CT):
                    for t in range(T):
                        o = slice(SEQ * c + P * t, SEQ * c + P * t + P)
                        mm(bank[7][:, o], sgsel[:, P * c:P * c + P], sgb[:, :], start=True, stop=False,
                           skip_group_check=True)
                        for j in range(2):
                            g = 2 * c + j
                            last = mm(bank[7][64 * j:64 * j + 64, o], v_n[:, t, 64 * g:64 * g + 64], sgw_t[:, g, :],
                                      start=False, stop=True, skip_group_check=True)
                last.then_inc(S("z_done"), 1)
                gate_block(2)
                gate_block(3)
                pe.wait_ge(S("p_done"), T * (l + 1))
                pe.wait_ge(S("ya_done"), l + 1)
                for h in range(NQ):
                    last = tp(bank[7][:, P * h:P * h + P], sc[0][:, h, :], ident[:, :])
                last.then_inc(S("p_tp"), 1)
                for i in range(2):
                    for j in range(4):
                        h, tk = 2 * i + j // 2, j % 2
                        last = tp(bank[4 + i][:, P * j:P * j + P], sc[1][:, h, P * tk:P * tk + P], ident[:, :])
                    last.then_inc(S("p_tp"), 1)
                gate_block(4)
                pe.wait_ge(S("p_t_done"), 3 * (l + 1))
                for h in range(NQ):
                    kv, r = h // 2, slice(64 * (h % 2), 64 * (h % 2) + 64)
                    vv = lambda t: qkv[:, t, (NH + kv) * HD:(NH + kv + 1) * HD]
                    o = SEQ * (h // 2)
                    mm(bank[6][r, o:o + P], vv(0), p_t[:, h, :], start=True, stop=True)
                    mm(bank[6][r, o + P:o + 2 * P], vv(0), p_t[:, 4 + 2 * h, :], start=True, stop=False)
                    last = mm(bank[6][r, o + P:o + 2 * P], vv(1), p_t[:, 5 + 2 * h, :], start=False, stop=True)
                last.then_inc(S("o_done"), 1)
                gate_block(5)
                gate_block(6)
                pe.wait_ge(S("conv_done"), l + 1)
                for c in range(CT):
                    last = mm(bank[4][:, 0:SEQ], ones[:, :], d_acc[:, c, :], start=c == 0, stop=c == CT - 1)
                last.then_inc(S("dsum_done"), 1)
                gate_block(7)
                pe.wait_ge(S("dsq_done"), l + 1)
                for c in range(CT):
                    last = mm(bank[5][:, 0:SEQ], ones[:, :], d_sig[:, c, :], start=c == 0, stop=c == CT - 1)
                last.then_inc(S("dvar_done"), 1)

                Y = [y_hi, y_lo]
                for n in range(NBR):
                    if n == 0:
                        pe.wait_ge(S("gates_done"), 16 * (l + 1))
                        pe.wait_ge(S("y_lo_done"), 4 * l + 1)
                    elif n == 1:
                        pe.wait_ge(S("y_lo_done"), 4 * l + 3)
                        pe.wait_ge(S("dv_done"), l + 1)
                    else:
                        pe.wait_ge(S("y_evac"), 16 * l + 4 * (n - 1))
                        if n == NBR - 1:
                            pe.wait_ge(S("y_lo_done"), 4 * (l + 1))
                    ready(at, Y0 + n)
                    wp = parts(at, Y0 + n, "p (c m) -> p c m", c=CT)
                    for i in range(4):
                        t, h = i // 2, i % 2
                        for c in range(CT):
                            last = three(bank[4 * (n % 2) + i][:, :],
                                         both(Y, n, slice(SEQ * c + P * t, SEQ * c + P * t + P)),
                                         both(wp, c, slice(512 * h, 512 * h + 512)), c == 0, c == CT - 1)
                        last.then_inc(S("y_job") if i < 3 else unit_used, 1)
                def merged_tp(t):
                    for k in range(KT):
                        if k % 4 == 0:
                            pe.wait_ge(S("m_add"), 12 * l + 8 + 2 * t + k // 4 + 1)
                        last = tp(bank[2 * t + k // 4][:, P * (k % 4):P * (k % 4) + P], merged[:, t, P * k:P * k + P],
                                  ident[:, :])
                        if k % 4 == 3:
                            last.then_inc(S("m_tp"), 1)

                def project(n, t):
                    _, k0, tiles = units_a[n]
                    pe.wait_ge(S("m_lo_done"), 4 * l + 2 * t + k0 // 4 + 1)
                    ready(at, n)
                    wp = parts(at, n, "p (c m) -> p c m", c=2)
                    for c in range(tiles):
                        k = k0 + c
                        for h in range(2):
                            last = three(bank[4 + 2 * t + h][:, :], both(H, k, slice(P * t, P * t + P)),
                                         both(wp, c, slice(512 * h, 512 * h + 512)), k == 0, k == KT - 1)
                    if t == T - 1:
                        last.then_inc(unit_used, 1)
                    elif n == NA - 1:
                        last.then_inc(S("o_half"), 1)

                merged_tp(0)
                project(O0, 0)
                merged_tp(1)
                project(O0 + 1, 0)
                project(O0, 1)
                project(O0 + 1, 1)
                for n in range(O0 + 2, NA - 2):
                    project(n, 0)
                    project(n, 1)
                project(NA - 2, 0)
                project(NA - 1, 0)
                project(NA - 2, 1)
                project(NA - 1, 1)

                pe.wait_ge(S("n2_xa"), l + 1)
                pe.wait_ge(S("n2_xd"), l + 1)
                for k in range(KT):
                    for t in range(T):
                        c = 256 * (k % 2) + P * t
                        last = tp(bank[4 + k // 2][:, c:c + P], xn[:, t, k, :], ident[:, :])
                    if k % 2:
                        last.then_inc(S("n2_t"), 1)
                pe.wait_ge(par_r, 16 * 5 * (l + 1))
                pe.wait_ge(S("h32_act"), 4 * (l + 1))
                pe.wait_ge(S("h32_dve"), 4 * (l + 1))
                for k in range(KT):
                    last = mm(bank[0][0:NR, 0:SEQ], wr[:, k, :], h32[:, k, :], start=k == 0, stop=k == KT - 1)
                last.then_inc(S("lt_done"), 1)
                pe.wait_ge(S("lt_sb"), l + 1)
                for t in range(T):
                    last = mm(bank[1][:, NR * t:NR * t + NR], lt[:, P * t:P * t + P], ident[0:NR, 0:NR], start=True, stop=True)
                last.then_inc(S("lg_tp"), 1)
                pe.wait_ge(S("goh_done"), l + 1)
                mm(bank[2][:, 0:NG], below[:, :], r4[:, 3, 0, :], start=True, stop=True)
                mm(bank[2][:, NG:2 * NG], below[:, :], r4[:, 3, 1, :], start=True, stop=False)
                mm(bank[2][:, NG:2 * NG], ones[:, :], r4[:, 3, 0, :], start=False, stop=True)
                mm(bank[2][:, 2 * NG:3 * NG], ones[:, :], r4[:, 3, 0, :], start=True, stop=False)
                mm(bank[2][:, 2 * NG:3 * NG], ones[:, :], r4[:, 3, 1, :], start=False, stop=True).then_inc(S("rank_done"), 1)
                pe.wait_ge(S("sel_done"), T * (l + 1))
                pe.wait_ge(S("xt_lo_done"), T * (l + 1))
                for k in range(KT):
                    if k >= 4:
                        pe.wait_ge(S("g_act"), KT * l + k - 4 + 1)
                    for i in range(2 * T):
                        last = mm(bank[4 + k % 4][:, :], (xt_hi, xt_lo)[i % 2][:, i // 2, k, :], sel[:, i // 2, :],
                                  start=i == 0, stop=i == 2 * T - 1)
                    last.then_inc(S("g_tp"), 1)
                    if k == 3:
                        pe.wait_ge(S("diag_done"), T * (l + 1))
                        mm(bank[3][:, 0:SEQ], ones[:, :], diag[:, :, :].rearrange("p t s -> p (t s)"), start=True,
                           stop=True).then_inc(S("posb_done"), 1)
                for i in range(4):
                    if i == 3:
                        pe.wait_ge(S("posb_read"), l + 1)
                    mm(bank[i][:, :], bsel[0:4, 4, :], bsel[0:4, 0:4, :].rearrange("p b s -> p (b s)"), start=True, stop=False,
                       skip_group_check=True)
                pe.wait_ge(S("g_act"), KT * (l + 1))
                pe.wait_ge(S("tab_ready"), l + 1)
                pe.wait_ge(S("cm_lo_done"), l + 1)
                for g in range(NG):
                    for t in range(T):
                        last = mm(bank[4][:, 16 * g:16 * g + 16], sel[:, t, P * g:P * g + P], cmr[:, t, :],
                                  start=t == 0, stop=t == T - 1)
                last.then_inc(S("cw_done"), 1)

                def scatter():
                    for i in range(4):
                        t, h = i // 2, i % 2
                        for zz in (z_hi, z_lo):
                            last = mm(bank[i][:, :], sel_t[:, P * t:P * t + P], zz[:, 512 * h:512 * h + 512],
                                      start=False, stop=zz is z_lo, skip_group_check=True)
                    last.then_inc(S("scattered"), 1)

                npass = pe.value_load(tab[0:1, 0, 6:7], min_val=NG, max_val=NG + 1)
                with pe.Fori(0, npass) as p:
                    PP = before + p
                    at = At(l, PP, True)
                    G = [g_hi, g_lo]
                    HD_ = [hd_hi, hd_lo]

                    def gate_up(e, h, n):
                        if e == 0:
                            pe.wait_ge(S("gp_lo"), 2 * (PP + l) + h + 1)
                        ready(at, n)
                        wp = parts(at, n, "p (w c f) -> p w c f", w=2, c=4)
                        for c in range(4):
                            k = 4 * h + c
                            last = three(bank[6 + e % 2][:, :].rearrange("p (w f) -> p w f", w=2), both(G, k),
                                         [w[:, :, c, :] for w in wp], k == 0, k == KT - 1)
                        last.then_inc(unit_used, 1)

                    def hidden_tp(e):
                        pe.wait_ge(S("hid_done"), EPG * PP + e + 1)
                        for f in range(FT):
                            last = tp(bank[6 + e % 2][:, P * f:P * f + P], hid[:, e % 2, P * f:P * f + P], ident[:, :])
                        last.then_inc(S("hid_tp"), 1)

                    def down(e, n):
                        ready(at, n)
                        pe.wait_ge(S("hd_lo_done"), EPG * PP + e + 1)
                        wp = parts(at, n, "p (c m) -> p c m", c=FT)
                        for h in range(2):
                            if e == EPG - 1 and h == 1:
                                last.then_inc(S("y_bank"), 1)
                            for f in range(FT):
                                last = three(bank[4 + h][:, :], both(HD_, e % 2, f), both(wp, f, slice(512 * h, 512 * h + 512)),
                                             e == 0 and f == 0, e == EPG - 1 and f == FT - 1)
                        last.then_inc(unit_used, 1)

                    gate_up(0, 0, 0)
                    gate_up(0, 1, 1)
                    gate_up(1, 0, 2)
                    hidden_tp(0)
                    gate_up(1, 1, 3)
                    pe.wait_ge(S("selt_done"), PP + l + 1)
                    down(0, 4)
                    gate_up(2, 0, 5)
                    hidden_tp(1)
                    gate_up(2, 1, 6)
                    down(1, 7)
                    gate_up(3, 0, 8)
                    hidden_tp(2)
                    gate_up(3, 1, 9)
                    down(2, 10)
                    hidden_tp(3)
                    scatter()
                    down(3, 11)
                pe.wait_ge(S("selt_done"), before + npass + l + 1)
                scatter()


_INS = ['x', 'positions', 'norm1_g', 'w_in', 'sgu_ln_g', 'sgu_ln_b', 'sgu_w', 'sgu_b', 'q_norm_g', 'k_norm_g', 'sinks',
        'conv3_w', 'conv31_w', 'conv31_b', 'cnorm_g', 'cnorm_b', 'w_branch', 'w_gate', 'b_gate', 'w_o',
        'norm2_g', 'w_group', 'b_group', 'w_expert', 'b_expert', 'w_e_gate', 'w_e_up', 'w_e_down']


def kernel(**inputs):
    import concourse.bacc as bacc
    from concourse.bass_utils import run_bass_kernel_spmd

    nc = bacc.Bacc("TRN2", target_bir_lowering=False, num_devices=1, dynamic_dma_scratch_size=1024)
    arrays, args = {}, []
    for name in _INS:
        a = np.ascontiguousarray(inputs[name])
        arrays[f"in_{name}"] = a
        args.append(nc.dram_tensor(f"in_{name}", a.shape, mybir.dt.from_np(a.dtype), kind="ExternalInput").ap())
    args.append(nc.dram_tensor("out_x", inputs["x"].shape, F32, kind="ExternalOutput").ap())
    trunk(nc, *args)
    r = run_bass_kernel_spmd(nc, [arrays], core_ids=[0])
    return r.results[0]["out_x"]
```
